# Optimizing a Trainium2 kernel written in Bass

```python
import math
import jax, jax.numpy as jnp
from jax import lax
import numpy as np

D_MODEL = 1024
BATCH = 1
SEQ = 1024
DEPTH = 1

SSM_GROUP = 16
SSM_STATE = 64
SSM_WIDTH = D_MODEL // 2
SSM_GROUPS = SSM_WIDTH // SSM_GROUP
HEAD_DIM = 64
ATTN_PATTERNS = ((128, 1), (512, 4), (2048, 16))
N_PATTERNS = len(ATTN_PATTERNS)
HEADS_PER_PATTERN = (D_MODEL // 2) // HEAD_DIM
N_ATTN_HEADS = N_PATTERNS * HEADS_PER_PATTERN
ATTN_WIDTH = N_ATTN_HEADS * HEAD_DIM
ATTN_OUT = HEADS_PER_PATTERN * HEAD_DIM
BLOCK = 128
N_IN = SSM_WIDTH + 3 * ATTN_WIDTH + 2 * D_MODEL
D_FF = 2816
CONV_WIDTH = 3
EPS = 1e-6

kernel_name = "hybrid_s5_dilated_attn_convffn"

def rmsnorm(t, g):
    tf = t.astype(jnp.float32)
    return tf * lax.rsqrt(jnp.mean(tf * tf, axis=-1, keepdims=True) + EPS) * g.astype(jnp.float32)

def alibi_slopes():
    i = np.arange(1, N_ATTN_HEADS + 1, dtype=np.float32)
    s = np.exp2(-8.0 * i / N_ATTN_HEADS).astype(np.float32)
    return jnp.asarray(s.reshape(HEADS_PER_PATTERN, N_PATTERNS).T)

def s5_scan(u, lam_re, lam_im, log_dt, b_re, b_im, c_re, c_im, d_skip):
    bsz, l, _ = u.shape
    u = u.astype(jnp.float32).reshape(bsz, l, SSM_GROUPS, SSM_GROUP)
    dt = jnp.exp(log_dt.astype(jnp.float32))[:, None]
    lr = lam_re.astype(jnp.float32)
    li = lam_im.astype(jnp.float32)
    mag = jnp.exp(lr * dt)
    ar = mag * jnp.cos(li * dt)
    ai = mag * jnp.sin(li * dt)
    den = lr * lr + li * li
    cr = ((ar - 1.0) * lr + ai * li) / den
    ci = (ai * lr - (ar - 1.0) * li) / den
    br = b_re.astype(jnp.float32)
    bi = b_im.astype(jnp.float32)
    bbar_re = cr[..., None] * br - ci[..., None] * bi
    bbar_im = cr[..., None] * bi + ci[..., None] * br
    bu_re = jnp.einsum('blgc,gpc->lbgp', u, bbar_re)
    bu_im = jnp.einsum('blgc,gpc->lbgp', u, bbar_im)
    a_re = jnp.broadcast_to(ar, (l, 1, SSM_GROUPS, SSM_STATE))
    a_im = jnp.broadcast_to(ai, (l, 1, SSM_GROUPS, SSM_STATE))

    def combine(e1, e2):
        a1r, a1i, b1r, b1i = e1
        a2r, a2i, b2r, b2i = e2
        return (a2r * a1r - a2i * a1i,
                a2r * a1i + a2i * a1r,
                a2r * b1r - a2i * b1i + b2r,
                a2r * b1i + a2i * b1r + b2i)

    _, _, x_re, x_im = lax.associative_scan(combine, (a_re, a_im, bu_re, bu_im), axis=0)
    y = (jnp.einsum('gcp,lbgp->blgc', c_re.astype(jnp.float32), x_re)
         - jnp.einsum('gcp,lbgp->blgc', c_im.astype(jnp.float32), x_im))
    return y.reshape(bsz, l, SSM_WIDTH) + d_skip.astype(jnp.float32) * u.reshape(bsz, l, SSM_WIDTH)

def dilated_window_attention(q, k, v, slopes, window, dilation):
    b, l, h, dh = q.shape
    n = l // dilation
    reach = window // dilation
    nb = -(-n // BLOCK)
    n_pad = nb * BLOCK

    def strided(t):
        t = t.reshape(b, n, dilation, h, dh).transpose(0, 2, 1, 3, 4)
        t = jnp.pad(t, ((0, 0), (0, 0), (0, n_pad - n), (0, 0), (0, 0)))
        return t.reshape(b, dilation, nb, BLOCK, h, dh)

    def with_prev(t):
        prev = jnp.pad(t, ((0, 0), (0, 0), (1, 0), (0, 0), (0, 0), (0, 0)))[:, :, :-1]
        return jnp.concatenate([prev, t], axis=3)

    qb = strided(q)
    kc = with_prev(strided(k))
    vc = with_prev(strided(v)).astype(jnp.float32)
    s = jnp.einsum('brnqhd,brnkhd->brnhqk', qb, kc).astype(jnp.float32)
    qi = jnp.arange(BLOCK)[:, None]
    ki = jnp.arange(2 * BLOCK)[None, :]
    delta = qi + BLOCK - ki
    key_idx = jnp.arange(nb)[:, None] * BLOCK - BLOCK + jnp.arange(2 * BLOCK)[None, :]
    valid = ((delta >= 0) & (delta <= reach))[None] & (key_idx >= 0)[:, None, :]
    bias = -slopes.astype(jnp.float32)[:, None, None] * (delta * dilation).astype(jnp.float32)[None]
    s = jnp.where(valid[None, None, :, None], s + bias[None, None, None], -jnp.inf)
    m = jnp.max(s, axis=-1, keepdims=True)
    p = jnp.exp(s - m)
    den = jnp.sum(p, axis=-1, keepdims=True)
    o = jnp.einsum('brnhqk,brnkhd->brnqhd', p, vc) / jnp.swapaxes(den, 3, 4)
    lse = jnp.swapaxes((m + jnp.log(den))[..., 0], 3, 4)
    o = o.reshape(b, dilation, n_pad, h, dh)[:, :, :n].transpose(0, 2, 1, 3, 4).reshape(b, l, h, dh)
    lse = lse.reshape(b, dilation, n_pad, h)[:, :, :n].transpose(0, 2, 1, 3).reshape(b, l, h)
    return o, lse

def causal_dwconv(t, w, bias):
    f = t.shape[-1]
    y = lax.conv_general_dilated(
        t.astype(jnp.float32), w.astype(jnp.float32)[:, None, :],
        window_strides=(1,), padding=[(w.shape[0] - 1, 0)],
        dimension_numbers=('NWC', 'WIO', 'NWC'), feature_group_count=f)
    return y + bias.astype(jnp.float32)

def setup_inputs(seed: int = 0) -> dict:
    key = jax.random.key(seed)
    ks = jax.random.split(key, 24)
    f32 = jnp.float32

    def nrm(k, shape, scale):
        return jax.random.normal(k, shape, f32) * scale

    gp = (DEPTH, SSM_GROUPS, SSM_STATE)
    return {
        'x': nrm(ks[0], (BATCH, SEQ, D_MODEL), 1.0),
        'norm_mix_g': 1.0 + nrm(ks[1], (DEPTH, D_MODEL), 0.02),
        'w_in': nrm(ks[2], (DEPTH, D_MODEL, N_IN), D_MODEL ** -0.5),
        'ssm_lambda_re': -0.5 * jnp.exp(nrm(ks[3], gp, 0.05)),
        'ssm_lambda_im': jnp.broadcast_to(jnp.pi * jnp.arange(SSM_STATE, dtype=f32), gp) + nrm(ks[4], gp, 0.01),
        'ssm_log_dt': jax.random.uniform(ks[5], (DEPTH, SSM_GROUPS), f32, math.log(1e-3), math.log(1e-1)),
        'ssm_b_re': nrm(ks[6], (DEPTH, SSM_GROUPS, SSM_STATE, SSM_GROUP), (2 * SSM_GROUP) ** -0.5),
        'ssm_b_im': nrm(ks[7], (DEPTH, SSM_GROUPS, SSM_STATE, SSM_GROUP), (2 * SSM_GROUP) ** -0.5),
        'ssm_c_re': nrm(ks[8], (DEPTH, SSM_GROUPS, SSM_GROUP, SSM_STATE), SSM_STATE ** -0.5),
        'ssm_c_im': nrm(ks[9], (DEPTH, SSM_GROUPS, SSM_GROUP, SSM_STATE), SSM_STATE ** -0.5),
        'ssm_d': nrm(ks[10], (DEPTH, SSM_WIDTH), 1.0),
        'glu_w_val': nrm(ks[11], (DEPTH, SSM_WIDTH, D_MODEL), SSM_WIDTH ** -0.5),
        'glu_w_gate': nrm(ks[12], (DEPTH, SSM_WIDTH, D_MODEL), SSM_WIDTH ** -0.5),
        'q_norm_g': 1.0 + nrm(ks[13], (DEPTH, HEAD_DIM), 0.02),
        'k_norm_g': 1.0 + nrm(ks[14], (DEPTH, HEAD_DIM), 0.02),
        'w_attn_up': nrm(ks[15], (DEPTH, ATTN_OUT, D_MODEL), ATTN_OUT ** -0.5),
        'w_out': nrm(ks[16], (DEPTH, D_MODEL, D_MODEL), D_MODEL ** -0.5),
        'norm_ffn_g': 1.0 + nrm(ks[17], (DEPTH, D_MODEL), 0.02),
        'ffn_w_gate': nrm(ks[18], (DEPTH, D_MODEL, D_FF), D_MODEL ** -0.5),
        'ffn_w_up': nrm(ks[19], (DEPTH, D_MODEL, D_FF), D_MODEL ** -0.5),
        'ffn_conv_w': nrm(ks[20], (DEPTH, CONV_WIDTH, D_FF), CONV_WIDTH ** -0.5),
        'ffn_conv_b': nrm(ks[21], (DEPTH, D_FF), 0.01),
        'ffn_w_down': nrm(ks[22], (DEPTH, D_FF, D_MODEL), D_FF ** -0.5),
    }

def reference(x, norm_mix_g, w_in, ssm_lambda_re, ssm_lambda_im, ssm_log_dt, ssm_b_re, ssm_b_im,
              ssm_c_re, ssm_c_im, ssm_d, glu_w_val, glu_w_gate, q_norm_g, k_norm_g, w_attn_up,
              w_out, norm_ffn_g, ffn_w_gate, ffn_w_up, ffn_conv_w, ffn_conv_b, ffn_w_down):
    b, l, _ = x.shape
    slopes = alibi_slopes()
    scale = HEAD_DIM ** -0.5
    for i in range(DEPTH):
        hmix = rmsnorm(x, norm_mix_g[i])
        proj = hmix @ w_in[i].astype(jnp.float32)
        o1 = SSM_WIDTH
        o2 = o1 + 3 * ATTN_WIDTH
        u_ssm = proj[..., :o1]
        qkv = proj[..., o1:o2].reshape(b, l, 3, N_PATTERNS, HEADS_PER_PATTERN, HEAD_DIM)
        gate_a = jax.nn.sigmoid(proj[..., o2:o2 + D_MODEL])
        gate_b = jax.nn.sigmoid(proj[..., o2 + D_MODEL:])

        y_ssm = jax.nn.gelu(s5_scan(u_ssm, ssm_lambda_re[i], ssm_lambda_im[i], ssm_log_dt[i],
                                    ssm_b_re[i], ssm_b_im[i], ssm_c_re[i], ssm_c_im[i], ssm_d[i]),
                            approximate=False)
        y_a = (y_ssm @ glu_w_val[i].astype(jnp.float32)) * jax.nn.sigmoid(y_ssm @ glu_w_gate[i].astype(jnp.float32))

        q = rmsnorm(qkv[:, :, 0], q_norm_g[i]) * scale
        k = rmsnorm(qkv[:, :, 1], k_norm_g[i])
        v = qkv[:, :, 2]
        outs = []
        lses = []
        for g, (window, dilation) in enumerate(ATTN_PATTERNS):
            o_g, lse_g = dilated_window_attention(q[:, :, g], k[:, :, g], v[:, :, g], slopes[g], window, dilation)
            outs.append(o_g)
            lses.append(lse_g)
        wgt = jax.nn.softmax(jnp.stack(lses, axis=0), axis=0)
        o_attn = jnp.sum(wgt[..., None] * jnp.stack(outs, axis=0), axis=0).reshape(b, l, ATTN_OUT)
        y_b = o_attn @ w_attn_up[i].astype(jnp.float32)

        mixed = (gate_a * y_a + gate_b * y_b) @ w_out[i].astype(jnp.float32)
        x = (x.astype(jnp.float32) + mixed).astype(x.dtype)

        hf = rmsnorm(x, norm_ffn_g[i])
        g_pre = causal_dwconv(hf @ ffn_w_gate[i].astype(jnp.float32), ffn_conv_w[i], ffn_conv_b[i])
        ff = (jax.nn.gelu(g_pre, approximate=False) * (hf @ ffn_w_up[i].astype(jnp.float32))) @ ffn_w_down[i].astype(jnp.float32)
        x = (x.astype(jnp.float32) + ff).astype(x.dtype)
    return x


_drawn_inputs = setup_inputs


def setup_inputs(seed=0):
    import zlib

    import numpy as np

    out = dict(_drawn_inputs(seed))
    spreads = {}
    factors = {'norm_mix_g': 6.747,
     'ssm_lambda_re': 8.0,
     'ssm_lambda_im': 2.804,
     'ssm_log_dt': 2.904,
     'ssm_b_re': 3.929,
     'ssm_b_im': 3.977,
     'ssm_c_re': 3.93,
     'ssm_c_im': 4.009,
     'q_norm_g': 8.0,
     'k_norm_g': 8.0,
     'norm_ffn_g': 3.701,
     'ffn_conv_b': 8.0}
    for name, (base, spread) in spreads.items():
        noise = np.random.default_rng([zlib.crc32(name.encode()), seed]).standard_normal(out[name].shape)
        drawn = base * np.exp(spread * noise) if base else spread * noise
        out[name] = __import__('jax').numpy.asarray(drawn.astype(out[name].dtype))
    for name, factor in factors.items():
        out[name] = (out[name] * factor).astype(out[name].dtype)
    return out
```

```python
from contextlib import ExitStack

import numpy as np

import concourse.bass as bass
from concourse import mybir

F32 = mybir.dt.float32
F32R = mybir.dt.float32r
I32 = mybir.dt.int32
ALU = mybir.AluOpType
ACT = mybir.ActivationFunctionType

P = 128
T = 1024
D = 1024
KC = D // P
HT = 512
DH = 64
HEADS = 8
HP = HEADS // 2
DIL = (1, 4, 16)
NPAT = len(DIL)
REACH = 128
NEG = -1e30
EPS = 1e-6
SSM_W = 512
NGROUP = 32
GC = 16
NST = 64
CH = 8
NCH = T // CH
GB = 8
FF = 2816
NF = FF // P
EXP_LN_SET = 6

B_A0, B_ALOOP, B_AEND = 0, 4, 34
B_E1, B_E2, B_F, B_G, B_D, B_END = 40, 56, 72, 80, 124, 146
G_E2, G_F, G_G, G_D = 112, 160, 176, 264


class Chain:

    def __init__(self, eng, sem):
        self.eng, self.sem, self.base, self.n = eng, sem, 0, 0

    def link(self, ins):
        self.n += 1
        ins.then_inc(self.sem, 1)
        self.eng.wait_ge(self.sem, self.base + self.n)

    def enter(self, i, per):
        self.start, self.per = self.base + self.n, per
        self.base, self.n = self.start + i * per, 0

    def leave(self, trips):
        assert self.n == self.per, f"steps of one iteration: {self.n}"
        self.base, self.n = self.start + trips * self.per, 0


def bass_hybrid_block(nc, xT, wblocks, wup, masks, consts, gmix, gffn, gqk, lam, bmat, cmat, dsk, cw, smallc, out):
    ctx = ExitStack()
    with ctx:
        def sem(name):
            return ctx.enter_context(nc.semaphore(name))

        def tensors(stack):
            return lambda name, shape, dt=F32: stack.enter_context(nc.sbuf_tensor(name, shape, dt))

        u_scr = nc.dram_tensor("u_scr", [SSM_W, T], F32).ap()
        y_scr = nc.dram_tensor("y_scr", [SSM_W, T], F32).ap()
        o_scr = nc.dram_tensor("o_scr", [HP, P, T], F32).ap()
        zb_scr = nc.dram_tensor("zb_scr", [KC, P, T], F32).ap()
        x1_scr = nc.dram_tensor("x1_scr", [KC, P, T], F32).ap()
        rt_scr = nc.dram_tensor("rt_scr", [P, 2, NGROUP, NCH + 1], F32).ap()

        sb = tensors(ctx)
        cst_s = sb("cst_s", [P, 3, P])
        ident, blk_ones, ones = cst_s[:, 0], cst_s[:, 1], cst_s[:, 2]
        small = sb("small", [P, 3])
        sgn, gns, epsc = small[:, 0:1], small[:, 1:2], small[:, 2:3]
        gm = sb("gm", [P, KC])
        gf = sb("gf", [P, KC])
        gq = sb("gq", [P, 2])
        dsk_s = sb("dsk_s", [P, HP])
        cws = sb("cws", [P, NF, 4])
        raw = [sb(f"raw{i}", [P, 1024]) for i in range(2)]
        whi = [sb(f"whi{i}", [P, 1024], F32R) for i in range(2)]
        wlo = [sb(f"wlo{i}", [P, 1024], F32R) for i in range(2)]
        ccr = sb("ccr", [P, NGROUP, CH])
        cci = sb("cci", [P, NGROUP, CH])
        g_a = sb("g_a", [P, NGROUP, CH + 1])
        g_b = sb("g_b", [P, NGROUP, CH + 1])
        g_c = sb("g_c", [P, NGROUP, CH + 1])
        g_d = sb("g_d", [P, NGROUP, CH + 1])
        mag8 = sb("mag8", [P, NGROUP])
        h_stack = ExitStack()
        sb = tensors(h_stack)
        hhi = sb("hhi", [P, KC, T], F32R)
        hlo = sb("hlo", [P, KC, T], F32R)

        with ExitStack() as s:
            sb = tensors(s)
            qn = [sb(f"qn{g}", [P, T]) for g in range(NPAT)]
            kn = [sb(f"kn{g}", [P, T]) for g in range(NPAT)]
            vv = [sb(f"vv{g}", [P, KC, P]) for g in range(NPAT)]
            vt = sb("vt", [P, T])
            sp = sb("sp", [P, 4, 2, 256])
            ptr = sb("ptr", [P, 2, HT])
            run_n = sb("run_n", [P, T])
            run_z = sb("run_z", [P, T])
            num = sb("num", [P, T])
            new_n = sb("new_n", [P, HT])
            ab = sb("ab", [P, 2, HT])
            t_num = sb("t_num", [P, HT])
            t_z = sb("t_z", [P, HT])
        with ExitStack() as s:
            sb = tensors(s)
            x0 = sb("x0", [P, KC, T])
            rs0 = sb("rs0", [P, T])
            sb("over_vt", [P, T])
            rtc = sb("rtc", [P, NGROUP, NCH + 1])
            rts = sb("rts", [P, NGROUP, NCH + 1])
        with ExitStack() as s:
            sb = tensors(s)
            sb("over_a", [P, 9 * T + T + 2 * T + 4 * T + 4 * HT + HT])
            mask = [sb(f"mask{g}", [P, 2, 256]) for g in range(NPAT)]
            sq = sb("sq", [P, 2, HT])
            rn = sb("rn", [P, 2, HT])
            mx = sb("mx", [P, 2])
            negm = sb("negm", [P, 8, 2])
            den = sb("den", [P, 8, 2])
            utmp = sb("utmp", [P, CH, NCH])
            rtmp = sb("rtmp", [P, 2, GB, NCH // 2])
            hx = sb("hx", [P, T])
            lam_s = sb("lam_s", [P, 3, NGROUP])
            pr = sb("pr", [P, 12, NGROUP])
            er = sb("er", [P, 9, NGROUP])
            ei = sb("ei", [P, 9, NGROUP])
            mg = sb("mg", [P, 9, NGROUP])
        with ExitStack() as s:
            sb = tensors(s)
            ohi = sb("ohi", [P, HP, T], F32R)
            olo = sb("olo", [P, HP, T], F32R)
            zb = sb("zb", [P, 2, T])
            sg = sb("sg", [P, 2, HT])
            b_in = sb("b_in", [P, 2, GB, GC])
            c_in = sb("c_in", [P, 2, GB, GC])
            ttmp = sb("ttmp", [P, GB, CH + 1, GC])
            tb = sb("tb", [P, GB, CH, GC])
            gg = sb("gg", [P, GB, CH + 1, GC])
            gp = sb("gp", [P, GB, CH, GC])
            w1 = sb("w1", [P, GB, P])
            w1p = sb("w1p", [P, GB, P])
            kt = sb("kt", [GC, GB, P])
            mm_ = sb("mm_", [P, GB, P])
            uu = sb("uu", [P, GB, NCH])
            rt = sb("rt", [P, 2, GB, NCH + 1])
            ww = sb("ww", [P, GB, NCH])
            wt = sb("wt", [P, GB, NCH])
            zz = sb("zz", [P, GB, NCH])
        with ExitStack() as s:
            sb = tensors(s)
            zt = sb("zt", [P, KC, T])
            sb("over_zb", [P, 2, T])
            yhi = sb("yhi", [P, HP, T], F32R)
            ylo = sb("ylo", [P, HP, T], F32R)
            sg2 = sb("sg2", [P, 4, HT])
            t2 = sb("t2", [P, 2, HT])
            yu = sb("yu", [P, 2, T])
            zb2 = sb("zb2", [P, T])
        with ExitStack() as s:
            sb = tensors(s)
            x1 = sb("x1", [P, KC, T])
            xin = sb("xin", [P, 2, T])
            sq1 = sb("sq1", [P, T])
            rs1 = sb("rs1", [P, T])
            hx1 = sb("hx1", [P, T])
        with ExitStack() as s:
            sb = tensors(s)
            ff = sb("ff", [P, NF, T])
            gbuf = sb("gbuf", [P, 2, T + 2])
            cv = sb("cv", [P, T])
        h_stack.close()
        with ExitStack() as s:
            sb = tensors(s)
            fhi = sb("fhi", [P, 2, T], F32R)
            flo = sb("flo", [P, 2, T], F32R)
            x1r = sb("x1r", [P, KC, T])
            osb = sb("osb", [P, KC // 2, T])

        stat = [hx[:], rtmp[:].rearrange("p a g k -> p (a g k)")]

        bank = [ctx.enter_context(nc.psum_tensor(f"bank{i}", [P, HT], F32)) for i in range(8)]
        b_proj, b_nb, b_s, b_t, b_o = bank[0:2], bank[2], bank[3:5], bank[5], bank[6:8]

        loaded = [sem(f"loaded{i}") for i in range(2)]
        hi_done, lo_done = sem("hi_done"), sem("lo_done")
        groups = sem("groups")
        const_in, lam_in, x_in = sem("const_in"), sem("lam_in"), [sem(f"x_in{i}") for i in range(KC)]
        dve_c, act_c, pool_c, waits = sem("dve_c"), sem("act_c"), sem("pool_c"), sem("waits")
        xsq_done, xss_used, rs_done, ssx_done = sem("xsq_done"), sem("xss_used"), sem("rs_done"), sem("ssx_done")
        prep_a, prep_b, h_done = sem("prep_a"), sem("prep_b"), sem("h_done")
        rt_out = sem("rt_out")
        rt_ready = sem("rt_ready")
        pev, sq_done, ss_done, rn_done, nrm_done = (sem(x) for x in ("pev", "sq_done", "ss_done", "rn_done", "nrm_done"))
        vt_done, vev_done = sem("vt_done"), sem("vev_done")
        s_done, smx_done, exp_done, t_done, tev, pv_done = (sem(x) for x in ("s_done", "smx_done", "exp_done", "t_done", "tev", "pv_done"))
        mask_in = [sem(f"mask_in{g}") for g in range(NPAT)]
        mt_done, dt_done, m_read, d_read, ab_exp, merged, stat_done = (
            sem(x) for x in ("mt_done", "dt_done", "m_read", "d_read", "ab_exp", "merged", "stat_done"))
        o_ready, o_out, o_free, u_out = sem("o_ready"), sem("o_out"), sem("o_free"), sem("u_out")

        o_in, osplit_hi, osplit = [sem(f"o_in{i}") for i in range(HP)], sem("osplit_hi"), sem("osplit")
        sg_done, zb_done = sem("sg_done"), sem("zb_done")
        zb_out = [sem(f"zb_out{i}") for i in range(2)]
        bc_in, tb_done, gt_done, gp_done = sem("bc_in"), sem("tb_done"), sem("gt_done"), sem("gp_done")
        tr_done, w1_done, kt_done, m_in = (sem(x) for x in ("tr_done", "w1_done", "kt_done", "m_in"))
        u_in, rt_in, v_done, state_done, y_done, y_ev, y_out = (
            sem(x) for x in ("u_in", "rt_in", "v_done", "state_done", "y_done", "y_ev", "y_out"))
        y_in, ydu, yg_done, ysplit_hi, ysplit = sem("y_in"), sem("ydu"), sem("yg_done"), sem("ysplit_hi"), sem("ysplit")
        sga_done, sgt_done, zb_in, z_done, zread = (sem(x) for x in ("sga_done", "sgt_done", "zb_in", "z_done", "zread"))
        zs_hi, zs_lo = sem("zs_hi"), sem("zs_lo")
        t2_done, kt_ev, ln_done = sem("t2_done"), sem("kt_ev"), sem("ln_done")
        xr_in = [sem(f"xr_in{i}") for i in range(2)]
        x1_done, x1_out, h2_hi = sem("x1_done"), sem("x1_out"), sem("h2_hi")
        hx_done, hhi_done, h_lo = sem("hx_done"), sem("hhi_done"), sem("h_lo")
        gcopy, cv_done, gelu_done, ff_done, pad_done = (sem(x) for x in ("gcopy", "cv_done", "gelu_done", "ff_done", "pad_done"))
        fs_hi, fs_lo, down_used = sem("fs_hi"), sem("fs_lo"), sem("down_used")
        down_done, x1r_in, out_ready, out_done = sem("down_done"), sem("x1r_in"), sem("out_ready"), sem("out_done")

        def half(ap, h):
            return ap[:, h * HT:(h + 1) * HT]

        def by_residue(ap, g, h):
            dil = DIL[g]
            n = T // dil
            return ap.rearrange("p (r i) -> p i r", r=dil)[:, h * n // 2:(h + 1) * n // 2, :]

        def natural(ap, g, h):
            dil = DIL[g]
            v = ap.rearrange("p (i r) -> p r i", r=dil)
            return half(ap, h).rearrange("p (r i) -> p r i", r=1) if dil == 1 else v[:, h * dil // 2:(h + 1) * dil // 2, :]

        def split2(ap, g):
            dil = DIL[g]
            return ap.rearrange("p (r i) -> p r i", r=1 if dil == 1 else dil // 2)

        def keys(g, s):
            return 0 if (g == 0 and s > 0) or (g == 1 and s % 2) else P

        def stage_a(eng, slot, ublock, enter=None, leave=None):
            ublock(0, 0)
            slot(0, 0, 1, None, None, None)
            with eng.Fori(0, HP - 1) as hp:
                if enter:
                    enter(hp)
                b = B_ALOOP + 10 * hp
                slot(3 * hp + 1, 1, b, 3 * hp, 0, hp)
                slot(3 * hp + 2, 2, b + 3, 3 * hp + 1, 1, hp)
                ublock(hp + 1, b + 6)
                slot(3 * hp + 3, 0, b + 7, 3 * hp + 2, 2, hp)
            if leave:
                leave(HP - 1)
            last = 3 * (HP - 1)
            slot(last + 1, 1, B_AEND, last, 0, HP - 1)
            slot(last + 2, 2, B_AEND + 3, last + 1, 1, HP - 1)
            slot(None, None, None, last + 2, 2, HP - 1)

        block = ctx.enter_context(nc.Block())

        @block.sync
        def _(sp_):
            def load(n, src, par, cols=1024, first=False):
                if not first:
                    sp_.wait_ge(lo_done, n - 1)
                sp_.dma_start(raw[par][:, 0:cols], src).then_inc(loaded[par], 16)

            for k in range(3):
                sp_.dma_start(x0[:, k, :], xT[k]).then_inc(x_in[k], 16)
            sp_.dma_start(lam_s[:], lam).then_inc(lam_in, 16)
            for dst, src in ((small, smallc), (cst_s, consts), (gm, gmix), (gf, gffn), (gq, gqk), (dsk_s, dsk), (cws, cw)):
                sp_.dma_start(dst[:], src).then_inc(const_in, 16)
            for k in range(3, KC):
                sp_.dma_start(x0[:, k, :], xT[k]).then_inc(x_in[k], 16)
            for n in range(2):
                load(n, wblocks[n], n, first=True)
            for g in range(NPAT):
                sp_.dma_start(mask[g][:], masks[g, 0]).then_inc(mask_in[g], 16)
            for n in range(2, 4):
                load(n, wblocks[n], n % 2)

            def save_u(hp):
                sp_.wait_ge(pev, 20 * hp + 2)
                sp_.dma_start(u_scr.rearrange("(q c) t -> q c t", c=P)[hp],
                              utmp[:].rearrange("p j k -> p (j k)")).then_inc(u_out, 16)

            save_u(0)
            with sp_.Fori(0, HP - 1) as hp:
                for b in range(10):
                    load(B_ALOOP + 10 * hp + b, wblocks[B_ALOOP + 10 * hp + b], b % 2)
                save_u(hp + 1)
            for n in range(B_AEND, B_E1):
                load(n, wblocks[n], n % 2)
            load(B_E1, wblocks[B_E1], 0)
            load(B_E1 + 1, wup[0], 1, HT)
            for q in range(HP):
                sp_.wait_ge(o_out, 16 * HP)
                if q >= 2:
                    sp_.wait_ge(osplit, q - 1)
                sp_.dma_start(zb[:, q % 2, :], o_scr[q]).then_inc(o_in[q], 16)
            sp_.wait_ge(u_out, 16 * HP)
            sp_.wait_ge(rt_out, 32)

            def load_bc(it):
                sp_.dma_start(b_in[:], bmat.rearrange("p a (b g) c -> b p a g c", g=GB)[it]).then_inc(bc_in, 16)
                sp_.dma_start(c_in[:], cmat.rearrange("p a (b g) c -> b p a g c", g=GB)[it]).then_inc(bc_in, 16)

            load_bc(0)

            def e1_small(it, first):
                if not first:
                    sp_.wait_ge(y_done, 2 * it)
                for n in range(CH):
                    sp_.dma_start(uu[GC * n:GC * (n + 1)],
                                  u_scr.rearrange("(b g c) (j k) -> j b c g k", g=GB, c=GC, k=NCH)[CH - 1 - n, it]).then_inc(u_in, 16)
                if not first:
                    sp_.wait_ge(state_done, it)
                sp_.dma_start(rt[:], rt_scr.rearrange("p a (b g) k -> b p a g k", g=GB)[it]).then_inc(rt_in, 16)

            def e1(it, first=False, last=False):
                e1_small(it, first)
                b = B_E1 + 4 * it
                if not last:
                    sp_.wait_ge(gp_done, it + 1)
                    load_bc(it + 1)
                load(b + 2, wblocks[B_E1 + 2 * it + 1], 0)
                load(b + 3, wup[2 * it + 1], 1, HT)
                if not last:
                    load(b + 4, wblocks[B_E1 + 2 * it + 2], 0)
                    load(b + 5, wup[2 * it + 2], 1, HT)
                else:
                    load(b + 4, wblocks[48], 0)
                    load(b + 5, wblocks[49], 1)
                for p in range(2):
                    sp_.wait_ge(zb_done, 4 * it + 2 * p + 4)
                    sp_.dma_start(zb_scr[2 * it + p], zb[:, p, :]).then_inc(zb_out[p], 16)

            e1(0, first=True)
            with sp_.Fori(1, 3) as it:
                e1(it)
            e1(3, last=True)
            for q in range(HP):
                sp_.wait_ge(y_out, 16 * CH * HP)
                if q:
                    sp_.wait_ge(ysplit, q)
                sp_.dma_start(yu[:, 0, :], y_scr.rearrange("(q c) t -> q c t", c=P)[q]).then_inc(y_in, 16)
                sp_.dma_start(yu[:, 1, :], u_scr.rearrange("(q c) t -> q c t", c=P)[q]).then_inc(y_in, 16)
            for p in range(2):
                sp_.wait_ge(zb_out[p], 64)
            sp_.wait_ge(ysplit, HP)
            with sp_.Fori(0, KC) as m:
                sp_.wait_ge(z_done, 2 * m + 2)
                sp_.dma_start(zb2[:], zb_scr[m]).then_inc(zb_in, 16)
                load(B_E2 + 2 * m + 2, wblocks[50 + 2 * m], 0)
                load(B_E2 + 2 * m + 3, wblocks[51 + 2 * m], 1)
            for p in range(2):
                sp_.dma_start(xin[:, p, :], xT[p]).then_inc(xr_in[p], 16)
            for m in range(2, KC):
                load(B_F + m, wblocks[64 + m], m % 2)
                sp_.wait_ge(x1_done, 2 * (m - 1) + 4)
                sp_.dma_start(xin[:, m % 2, :], xT[m]).then_inc(xr_in[m % 2], 16)
            load(B_G, wblocks[72], 0)
            load(B_G + 1, wblocks[73], 1)
            for m in range(KC):
                sp_.wait_ge(x1_done, 2 * (m + 1) + 4)
                sp_.dma_start(x1_scr[m], x1[:, m, :]).then_inc(x1_out, 16)
            sp_.wait_ge(x1_out, 16 * KC)
            with sp_.Fori(0, NF // 2) as f2:
                for b in range(4):
                    load(B_G + 2 + 4 * f2 + b, wblocks[74 + 4 * f2 + b], b % 2)
            sp_.wait_ge(groups, G_D)
            for m in range(KC):
                sp_.dma_start(x1r[:, m, :], x1_scr[m]).then_inc(x1r_in, 16)
            with sp_.Fori(0, 10) as j:
                load(B_D + 2 + 2 * j, wblocks[118 + 2 * j], 0)
                load(B_D + 3 + 2 * j, wblocks[119 + 2 * j], 1)

        @block.gpsimd
        def _(pool):
            chain = Chain(pool, pool_c)

            def lo(n, par, cols=1024):
                pool.wait_ge(hi_done, n + 1)
                pool.tensor_tensor(wlo[par][:, 0:cols], raw[par][:, 0:cols], whi[par][:, 0:cols].bitcast(F32),
                                   ALU.subtract).then_inc(lo_done, 1)

            lo(0, 0)

            def ublock(hp, n):
                lo(n + 1, 1)

            def slot(n, g, b, a, ag, hp):
                par0 = {0: 1, 1: 0, 2: 1}.get(g)
                for j in range(12):
                    if n is not None and j % 4 == 0:
                        k = j // 4 + 1
                        lo(b + k, (par0 + k) % 2)
                    if n is not None and j in (3, 5, 7, 9):
                        gi = (j - 3) // 2
                        pool.wait_ge(rn_done, 4 * n + gi + 1)
                        pool.wait_ge(pev, 2 * (b + gi // 2) + gi % 2 + 1)
                        dst = by_residue((qn if gi < 2 else kn)[g][:, :], g, gi % 2)
                        src = rn[:, gi % 2, :].rearrange("p (i r) -> p i r", r=DIL[g])
                        pool.tensor_tensor(dst, dst, src, ALU.mult).then_inc(nrm_done, 1)
                    if a is not None and ag > 0 and j in (10, 11):
                        h = j - 10
                        nm, nz = (natural(x[:, :], ag, h) for x in (num, run_z))
                        e0 = split2(ab[:, 0, :], ag)
                        pool.wait_ge(ab_exp, hpc(hp, ag) + h + 1)
                        chain.link(pool.tensor_tensor(nm, nm, e0, ALU.mult))
                        chain.link(pool.tensor_tensor(nz, nz, e0, ALU.mult))
                        pool.wait_ge(d_read, 2 * a + h + 2)
                        chain.link(pool.tensor_tensor(nm, nm, split2(t_num[:, :], ag), ALU.add))
                        pool.tensor_tensor(nz, nz, split2(t_z[:, :], ag), ALU.add).then_inc(merged, 1)
                if a is None:
                    pool.wait_ge(rt_ready, 1)
                    pool.dma_start(rt_scr[:, 0], rtc[:]).then_inc(rt_out, 16)
                    pool.dma_start(rt_scr[:, 1], rts[:]).then_inc(rt_out, 16)
                if a is not None and ag == NPAT - 1:
                    pool.wait_ge(o_ready, hp + 1)
                    pool.dma_start(o_scr[hp], num[:]).then_inc(o_out, 16)
                    pool.wait_ge(o_out, 16 * (hp + 1))
                    pool.sem_inc(o_free, 1)

            def hpc(hp, ag):
                return 4 * hp + 2 * (ag - 1)

            pool.sem_inc(merged, 1)
            stage_a(pool, slot, ublock, lambda hp: chain.enter(hp, 12), chain.leave)

            def tb_table(it):
                pool.wait_ge(bc_in, 32 * (it + 1))
                cr, ci = (x.rearrange("p (b g) n -> p b g n", g=GB)[:, it].unsqueeze(3).broadcast_to([P, GB, CH, GC])
                          for x in (ccr[:], cci[:]))
                b0, b1 = (b_in[:, i].unsqueeze(2).broadcast_to([P, GB, CH, GC]) for i in range(2))
                chain.link(pool.tensor_tensor(tb[:], cr, b0, ALU.mult))
                chain.link(pool.tensor_tensor(ttmp[:, :, 0:CH], ci, b1, ALU.mult))
                chain.link(pool.tensor_tensor(tb[:], tb[:], ttmp[:, :, 0:CH], ALU.add))
                pool.sem_inc(tb_done, 1)

            def c_table(it, dst, x, y, lo_, n, done):
                cr, ci = (q.rearrange("p (b g) n -> p b g n", g=GB)[:, it][:, :, lo_:].unsqueeze(3).broadcast_to([P, GB, n, GC])
                          for q in (x[:], y[:]))
                c0, c1 = (c_in[:, i].unsqueeze(2).broadcast_to([P, GB, n, GC]) for i in range(2))
                chain.link(pool.tensor_tensor(dst[:], cr, c0, ALU.mult))
                chain.link(pool.tensor_tensor(ttmp[:, :, 0:n], ci, c1, ALU.mult))
                chain.link(pool.tensor_tensor(dst[:], dst[:], ttmp[:, :, 0:n], ALU.add))
                pool.sem_inc(done, 1)

            def g_table(it):
                c_table(it, gg, g_a, g_b, 0, CH + 1, gt_done)

            def gp_table(it):
                c_table(it, gp, g_c, g_d, 1, CH, gp_done)

            pool.wait_ge(prep_b, 2)
            tb_table(0)
            g_table(0)
            gp_table(0)

            def e1(it, last=False):
                b = B_E1 + 4 * it
                lo(b + 1, 1, HT)
                if not last:
                    pool.wait_ge(kt_done, it + 1)
                    tb_table(it + 1)
                lo(b + 2, 0)
                lo(b + 3, 1, HT)
                if not last:
                    pool.wait_ge(y_done, 2 * it + 2)
                    g_table(it + 1)
                lo(b + 4, 0)
                if not last:
                    gp_table(it + 1)

            e1(0)
            with pool.Fori(1, 3) as it:
                chain.enter(it - 1, 9)
                e1(it)
            chain.leave(2)
            e1(3, last=True)
            pool.sem_inc(z_done, 2)
            for q in range(HP):
                pool.wait_ge(ysplit_hi, q + 1)
                pool.tensor_tensor(ylo[:, q, :], zb2[:], yhi[:, q, :].bitcast(F32), ALU.subtract).then_inc(ysplit, 1)
            with pool.Fori(0, KC) as m:
                chain.enter(m, 2)
                lo(B_E2 + 2 * m + 1, 1)
                lo(B_E2 + 2 * m + 2, 0)
                pool.wait_ge(zb_in, 16 * (m + 1))
                for h in range(2):
                    pool.wait_ge(sga_done, 2 * m + h + 3)
                    pool.wait_ge(t2_done, 2 * m + h + 3)
                    chain.link(pool.tensor_tensor(t2[:, h, :], t2[:, h, :], sg2[:, h, :], ALU.mult))
                    pool.tensor_tensor(half(zt[:, m, :], h), t2[:, h, :], half(zb2[:], h), ALU.add).then_inc(z_done, 1)
            chain.leave(KC)
            with pool.Fori(0, KC // 2) as m2:
                lo(B_F + 2 * m2 + 1, 1)
                lo(B_F + 2 * m2 + 2, 0)
            with pool.Fori(0, NF // 2) as f2:
                for b in range(4):
                    lo(B_G + 4 * f2 + b + 1, (b + 1) % 2)
            with pool.Fori(0, 10) as j:
                lo(B_D + 2 * j + 1, 1)
                lo(B_D + 2 * j + 2, 0)
            lo(B_END - 1, 1)

        @block.tensor
        def _(pe):
            def mm3(ps, par, w0, k_list, hi, lo_, h, start, stop):
                for k in k_list:
                    c = w0(k)
                    a, b, x, y = whi[par][:, c:c + P], wlo[par][:, c:c + P], half(hi[:, k, :], h), half(lo_[:, k, :], h)
                    nc.tensor.matmul(ps, a, x, start=start and k == k_list[0], stop=False)
                    nc.tensor.matmul(ps, a, y, start=False, stop=False)
                    last = nc.tensor.matmul(ps, b, x, start=False, stop=stop and k == k_list[-1])
                return last

            def cols(k):
                return k * P

            def ready(n):
                pe.wait_ge(lo_done, n + 1)

            pe.wait_ge(const_in, 16 * 7)
            for k in range(KC):
                pe.wait_ge(xsq_done, k + 1)
                sqk = (sq, rn)[k % 2]
                for h in range(2):
                    m_ = nc.tensor.matmul(bank[h][:], ones, sqk[:, h, :], start=k == 0, stop=k == KC - 1)
                m_.then_inc(ssx_done, 1)

            def ublock(hp, n):
                ready(n)
                for h in range(2):
                    if isinstance(n, int):
                        pe.wait_ge(rs_done, 2)
                    else:
                        pe.wait_ge(pev, 2 * n + h - 1)
                    for k in range(KC):
                        if isinstance(n, int) and h == 0:
                            pe.wait_ge(h_lo, k + 1)
                        last = mm3(b_proj[h][:], 0, cols, [k], hhi, hlo, h, k == 0, k == KC - 1)
                    last.then_inc(groups, 1)

            def slot(n, g, b, a, ag, hp):
                par0 = {0: 1, 1: 0, 2: 1}.get(g)
                for j in range(12):
                    if n is not None:
                        blk, h, part = j // 4, j // 2 % 2, j % 2
                        if part == 0:
                            if h == 0:
                                ready(b + blk)
                            pe.wait_ge(pev, 2 * (b + blk) + h - 1)
                            if blk:
                                pe.wait_ge(sq_done, 4 * n + 2 * (blk - 1) + h + 1)
                        last = mm3(b_proj[h][:], (par0 + blk) % 2, cols, range(4 * part, 4 * part + 4), hhi, hlo, h,
                                   part == 0, part == 1)
                        if part == 1:
                            last.then_inc(groups, 1)
                    if a is not None:
                        if j in (0, 1):
                            if j == 0:
                                pe.wait_ge(m_read, 2 * a + 1)
                                pe.wait_ge(ln_done, 4 * a + 4)
                                pe.wait_ge(pev, vgroups(ag, hp))
                            else:
                                pe.wait_ge(vev_done, 2 * a + 1)
                            for c in range(4):
                                last = nc.tensor.transpose(b_nb[:, c * P:(c + 1) * P], vt[:, (4 * j + c) * P:(4 * j + c + 1) * P], ident)
                            last.then_inc(vt_done, 1)
                        if j < 8:
                            s0 = keys(ag, j)
                            if j == 0:
                                pe.wait_ge(nrm_done, 4 * a + 4)
                            else:
                                pe.wait_ge(smx_done, 8 * a + j)
                            for x in range(2):
                                r = slice(DH * x, DH * (x + 1))
                                last = nc.tensor.matmul(b_s[x][:, 256 * (j % 2) + s0:256 * (j % 2) + 256], qn[ag][r, j * P:(j + 1) * P],
                                                        kn[ag][r, (j - 1) * P + s0:(j + 1) * P], start=True, stop=True)
                            last.then_inc(s_done, 1)
                        if 2 <= j < 10:
                            s_ = j - 2
                            pe.wait_ge(exp_done, 8 * a + s_ + 1)
                            if s_ == 0:
                                pe.wait_ge(d_read, 2 * a + 1)
                            else:
                                pe.wait_ge(tev, 8 * a + s_)
                            for x in range(2):
                                for kb in range(keys(ag, s_) // P, 2):
                                    c = (2 * x + kb) * P
                                    last = nc.tensor.transpose(b_t[:, c:c + P], sp[:, s_ % 4, x, kb * P:(kb + 1) * P], ident)
                            last.then_inc(t_done, 1)
                        if 3 <= j < 11:
                            s_ = j - 3
                            if s_ == 0:
                                pe.wait_ge(vev_done, 2 * a + 2)
                            pe.wait_ge(tev, 8 * a + s_ + 1)
                            k0 = keys(ag, s_) // P
                            for x in range(2):
                                r = slice(DH * x, DH * (x + 1))
                                for kb in range(k0, 2):
                                    c = (2 * x + kb) * P
                                    last = nc.tensor.matmul(b_o[s_ // 4][r, (s_ % 4) * P:(s_ % 4 + 1) * P], vv[ag][:, s_ - 1 + kb, r],
                                                            ptr[:, s_ % 2, c:c + P], start=kb == k0, stop=kb == 1)
                            last.then_inc(pv_done, 1)
                    if n is not None and j in (2, 4, 6, 8):
                        gi = (j - 2) // 2
                        pe.wait_ge(sq_done, 4 * n + gi + 1)
                        if gi == 0:
                            if a is not None:
                                pe.wait_ge(vev_done, 2 * a + 2)
                        else:
                            pe.wait_ge(ln_done, 4 * n + gi)
                        nc.tensor.matmul(b_nb[:], blk_ones, sq[:, gi % 2, :], start=True, stop=True).then_inc(ss_done, 1)
                    if a is not None and j in (9, 11):
                        h = (j - 9) // 2
                        pe.wait_ge(stat_done, 2 * a + h + 1)
                        if h:
                            pe.wait_ge(m_read, 2 * a + 2)
                        elif n is not None:
                            pe.wait_ge(ln_done, 4 * n + 4)
                        for s_ in range(4):
                            last = nc.tensor.transpose(b_nb[:, s_ * P:(s_ + 1) * P], stat[h][:, s_ * P:(s_ + 1) * P], ident)
                        last.then_inc(mt_done, 1)
                    if a is not None and j in (10, 11):
                        h = j - 10
                        if h:
                            pe.wait_ge(d_read, 2 * a + 2)
                        else:
                            pe.wait_ge(tev, 8 * a + 8)
                        for s_ in range(4):
                            last = nc.tensor.transpose(b_t[:, s_ * P:(s_ + 1) * P], stat[h][:, HT + s_ * P:HT + (s_ + 1) * P], ident)
                        last.then_inc(dt_done, 1)

            def vgroups(ag, hp):
                return 20 * hp + {0: 8, 1: 14, 2: 20}[ag]

            stage_a(pe, slot, ublock)

            def e1(it, first=False):
                for step in range(12):
                    p, q = step // 6, step % 6
                    m = 2 * it + p
                    n = B_E1 + 4 * it + 2 * p
                    if q == 0:
                        ready(n)
                    if q == 4:
                        ready(n + 1)
                        if first and p == 0:
                            pe.wait_ge(osplit, HP)
                    if q < 4:
                        h, part = q // 2, q % 2
                        if part == 0:
                            pe.wait_ge(sg_done, 2 * m + h + 1)
                        last = mm3(bank[h][:], 0, cols, range(4 * part, 4 * part + 4), hhi, hlo, h, part == 0, part == 1)
                        if part:
                            last.then_inc(groups, 1)
                    else:
                        h = q - 4
                        pe.wait_ge(zb_done, 2 * m + h + 1)
                        mm3(bank[2 + h][:], 1, cols, range(HP), ohi, olo, h, True, True).then_inc(groups, 1)
                    if step == 0:
                        pe.wait_ge(tb_done, it + 1)
                        if not first:
                            pe.wait_ge(y_ev, 2 * it)
                        for sub in range(2):
                            for q4 in range(4):
                                gl = 4 * sub + q4
                                last = nc.tensor.transpose(bank[4 + sub][:, q4 * P:(q4 + 1) * P], tb[:, gl].rearrange("p n c -> p (n c)"), ident)
                            last.then_inc(tr_done, 1)
                        pe.wait_ge(gt_done, it + 1)
                        for sub in range(2):
                            for q4 in range(4):
                                gl = 4 * sub + q4
                                last = nc.tensor.matmul(bank[6 + sub][0:GC, q4 * P:(q4 + 1) * P], tb[:, gl, 0, :],
                                                        gg[:, gl, 0:CH].rearrange("p n c -> p (n c)"), start=True, stop=True)
                        last.then_inc(kt_done, 1)
                    if step == 3:
                        pe.wait_ge(w1_done, 2 * it + 2)
                        pe.wait_ge(kt_ev, it + 1)
                        pe.wait_ge(u_in, 16 * CH * (it + 1))
                        for sub in range(2):
                            for q4 in range(4):
                                gl = 4 * sub + q4
                                nc.tensor.matmul(bank[4 + 2 * sub][:, q4 * P:(q4 + 1) * P], w1[:, gl], uu[:, gl], start=True, stop=True)
                                last = nc.tensor.matmul(bank[5 + 2 * sub][:, q4 * P:(q4 + 1) * P], w1p[:, gl], uu[:, gl], start=True, stop=True)
                            last.then_inc(v_done, 1)
                    if step == 8:
                        pe.wait_ge(state_done, it + 1)
                        pe.wait_ge(m_in, 16 * CH * (it + 1))
                        pe.wait_ge(gp_done, it + 1)
                        for sub in range(2):
                            for q4 in range(4):
                                gl = 4 * sub + q4
                                ps = bank[4 + sub][:, q4 * P:(q4 + 1) * P]
                                nc.tensor.matmul(ps, mm_[:, gl], uu[:, gl], start=True, stop=False)
                                nc.tensor.matmul(ps, gg[:, gl, 1:].rearrange("p n c -> p (n c)"), ww[:, gl], start=False, stop=False)
                                last = nc.tensor.matmul(ps, gp[:, gl].rearrange("p n c -> p (n c)"), wt[:, gl], start=False, stop=True)
                            last.then_inc(y_done, 1)

            pe.wait_ge(d_read, 2 * 12 + 1)
            e1(0, first=True)
            with pe.Fori(1, 3) as it:
                e1(it)
            e1(3)

            with pe.Fori(0, KC) as m:
                n = B_E2 + 2 * m
                ready(n)
                for h in range(2):
                    pe.wait_ge(sga_done, 2 * m + h + 1)
                    mm3(bank[h][:], 0, cols, range(KC), hhi, hlo, h, True, True).then_inc(groups, 1)
                ready(n + 1)
                pe.wait_ge(ysplit, HP)
                for w in range(2):
                    for h in range(2):
                        pe.wait_ge(t2_done, 2 * m + h + 1)
                        mm3(bank[2 + 2 * w + h][:], 1, lambda k: (4 * w + k) * P, range(HP), yhi, ylo, h, True, True).then_inc(groups, 1)

            with pe.Fori(0, KC // 2) as m2:
                for p in range(2):
                    ready(B_F + 2 * m2 + p)
                    for h in range(2):
                        pe.wait_ge(x1_done, 4 * m2 + 2 * p + h + 1)
                        for k in range(KC):
                            if p == 0 and h == 0:
                                pe.wait_ge(zs_lo, k + 1)
                            last = mm3(bank[2 * p + h][:], p, cols, [k], hhi, hlo, h, k == 0, k == KC - 1)
                        last.then_inc(groups, 1)

            for k in range(KC):
                pe.wait_ge(xsq_done, KC + k + 1)
                for h in range(2):
                    m_ = nc.tensor.matmul(bank[4 + h][:], ones, half((sq1, hx1)[k % 2][:], h), start=k == 0, stop=k == KC - 1)
                m_.then_inc(ssx_done, 1)

            with pe.Fori(0, NF // 2) as f2:
                for p in range(2):
                    n = B_G + 4 * f2 + 2 * p
                    for w in range(2):
                        ready(n + w)
                        for h in range(2):
                            pe.wait_ge((gcopy, ff_done)[w], 4 * f2 + 2 * p + h + 1)
                            for k in range(KC):
                                if p == w == h == 0:
                                    pe.wait_ge(h_lo, KC + k + 1)
                                last = mm3(bank[4 * p + 2 * w + h][:], w, cols, [k], hhi, hlo, h, k == 0, k == KC - 1)
                            last.then_inc(groups, 1)

            def down(idx, par, start=False, stop=False, free=None):
                ready(B_D + idx)
                for c in range(2):
                    pe.wait_ge(fs_lo, 2 * idx + c + 1)
                    for m in range(4):
                        for h in range(2):
                            if free and c == 0:
                                pe.wait_ge(out_ready, 2 * m + h + 1)
                            last = mm3(bank[2 * m + h][:], par, lambda k: c * HT + m * P, [c], fhi, flo, h,
                                       start and c == 0, stop and c == 1)
                    last.then_inc((down_used, groups)[c], 1)

            pe.wait_ge(ff_done, 2 * NF + 4)
            for mh in range(2):
                i0 = 11 * mh
                down(i0, mh, start=True, free=mh)
                with pe.Fori(0, 4) as j:
                    for q in range(2):
                        down(i0 + 1 + 2 * j + q, (mh + 1 + q) % 2)
                down(i0 + 9, (mh + 1) % 2)
                down(i0 + 10, mh, stop=True)

        @block.scalar
        def _(act):
            def exp_ln_set():
                act.add_instruction(mybir.InstLoadActFuncSet(
                    name=nc.get_next_instruction_name(), engine=act.engine, act_func_set_id=EXP_LN_SET))

            chain = Chain(act, act_c)
            exp_ln_set()
            act.wait_ge(lam_in, 16)
            act.activation(pr[:, 0], lam_s[:, 2], ACT.Exp).then_inc(prep_a, 1)
            act.wait_ge(prep_b, 1)
            for n in range(1, 9):
                act.activation(mg[:, n], pr[:, 1], ACT.Exp, scale=float(n))
            act.activation(pr[:, 6], pr[:, 4], ACT.Sin)
            act.activation(pr[:, 7], pr[:, 5], ACT.Sin).then_inc(prep_a, 1)
            exp_ln_set()

            def norm(which, src, sqb, rs, b0, hxb):
                for k in range(KC):
                    if which == 0:
                        act.wait_ge(x_in[k], 16)
                    else:
                        act.wait_ge(x1_done, 2 * k + 2 + 4)
                    if k >= 2:
                        act.wait_ge(ssx_done, KC * which + k - 1)
                    act.activation(sqb[k % 2], src[:, k, :], ACT.Square).then_inc(xsq_done, 1)
                act.wait_ge(ssx_done, KC * (which + 1))
                for h in range(2):
                    chain.link(act.activation(half(rs[:], h), bank[b0 + h][:], ACT.Ln, scale=1.0 / D, bias=epsc))
                    act.activation(half(rs[:], h), half(rs[:], h), ACT.Exp, scale=-0.5).then_inc(rs_done, 1)
                for k in range(KC):
                    act.wait_ge(hx_done, KC * which + k + 1)
                    act.activation(hhi[:, k, :], hxb[k % 2], ACT.Copy).then_inc(hhi_done, 1)

            act.wait_ge(const_in, 16 * 7)
            norm(0, x0, [x[:].rearrange("p a t -> p (a t)") for x in (sq, rn)], rs0, 0,
                 [hx[:], utmp[:].rearrange("p j k -> p (j k)")])

            def ublock(hp, n):
                pass

            def slot(n, g, b, a, ag, hp):
                for j in range(12):
                    if n is not None and j % 2 and j < 8:
                        gi = j // 2
                        act.wait_ge(groups, 2 * (b + gi // 2) + gi % 2 + 1)
                        if gi >= 2:
                            act.wait_ge(ss_done, 4 * n + gi - 1)
                        act.activation(sq[:, gi % 2, :], b_proj[gi % 2][:], ACT.Square).then_inc(sq_done, 1)
                    if a is not None and 2 <= j < 10:
                        s_ = j - 2
                        act.wait_ge(t_done, 8 * a + s_ + 1)
                        src, dst = (x.rearrange("p (h q) -> p h q", h=2)[:, :, keys(ag, s_):] for x in (b_t[:], ptr[:, s_ % 2, :]))
                        act.activation(dst, src, ACT.Copy).then_inc(tev, 1)
                    if n is not None and j in (2, 4, 6, 8):
                        gi = (j - 2) // 2
                        act.wait_ge(ss_done, 4 * n + gi + 1)
                        if not isinstance(n, int) or n or gi >= 2:
                            act.wait_ge(nrm_done, 4 * n + gi - 1)
                        act.activation(rn[:, gi % 2, :], b_nb[:], ACT.Ln, scale=1.0 / DH, bias=epsc).then_inc(ln_done, 1)
                        act.wait_ge(ln_done, 4 * n + gi + 1)
                        act.activation(rn[:, gi % 2, :], rn[:, gi % 2, :], ACT.Exp, scale=-0.5).then_inc(rn_done, 1)
                    if a is not None and j < 8:
                        act.wait_ge(smx_done, 8 * a + j + 1)
                        s0 = keys(ag, j)
                        for x in range(2):
                            last = act.activation(sp[:, j % 4, x, s0:], sp[:, j % 4, x, s0:], ACT.Exp,
                                                  bias=negm[:, j, x:x + 1], accum_out=den[:, j, x:x + 1])
                        last.then_inc(exp_done, 1)
                    if a is not None and j == 8 and not isinstance(hp, int):
                        act.dma_start(mask[ag][:], masks[ag, hp + 1]).then_inc(mask_in[ag], 16)
                    if a is not None and ag and j >= 10:
                        h = j - 10
                        act.wait_ge(m_read, 2 * a + h + 2)
                        act.activation(ab[:], ab[:], ACT.Exp).then_inc(ab_exp, 1)

            stage_a(act, slot, ublock)

            def e1(it, first=False):
                if not first:
                    act.wait_ge(y_out, 16 * CH * it)
                for sub in range(2):
                    act.wait_ge(tr_done, 2 * it + sub + 1)
                    v = bank[4 + sub][:].rearrange("p (g s) -> p g s", s=P)
                    r = slice(4 * sub, 4 * sub + 4)
                    act.activation(w1[:, r], v, ACT.Copy)
                    act.activation(w1p[:, r, 0:NST], v[:, :, NST:], ACT.Copy)
                    act.activation(w1p[:, r, NST:], v[:, :, 0:NST], ACT.Copy, scale=-1.0).then_inc(w1_done, 1)
                act.wait_ge(kt_done, it + 1)
                act.activation(kt[:, 0:4], bank[6][0:GC, :].rearrange("p (g s) -> p g s", s=P), ACT.Copy)
                act.activation(kt[:, 4:8], bank[7][0:GC, :].rearrange("p (g s) -> p g s", s=P), ACT.Copy).then_inc(kt_ev, 1)
                act.wait_ge(kt_ev, it + 1)
                for n in range(CH):
                    j = CH - 1 - n
                    act.dma_start(mm_[GC * n:GC * (n + 1), :, GC * j:], kt[:, :, 0:P - GC * j]).then_inc(m_in, 16)
                for p in range(2):
                    m = 2 * it + p
                    for h in range(2):
                        act.wait_ge(groups, 2 * (B_E1 + 4 * it + 2 * p) + h + 1)
                        act.wait_ge(zb_done, 2 * m + h + 1)
                        act.activation(sg[:, h, :], bank[h][:], ACT.Sigmoid).then_inc(sg_done, 1)
                    if p == 1:
                        for sub in range(2):
                            act.wait_ge(y_done, 2 * it + sub + 1)
                            act.activation(w1p[:, 4 * sub:4 * sub + 4], bank[4 + sub][:].rearrange("p (g s) -> p g s", s=P),
                                           ACT.Copy).then_inc(y_ev, 1)
                        act.wait_ge(y_ev, 2 * it + 2)
                        for i in range(CH):
                            act.dma_start(y_scr.rearrange("(b g c) (i k) -> i b c g k", g=GB, c=GC, k=NCH)[i, it],
                                          w1p[GC * i:GC * (i + 1)]).then_inc(y_out, 16)

            act.sem_inc(sg_done, 2)
            e1(0, first=True)
            with act.Fori(1, 3) as it:
                e1(it)
            e1(3)
            act.sem_inc(sga_done, 2)
            for q in range(HP):
                act.wait_ge(ydu, q + 1)
                if q:
                    act.wait_ge(ysplit, q)
                act.activation(zb2[:].rearrange("p (k i) -> p i k", i=CH), yu[:, 0, :].rearrange("p (i k) -> p i k", i=CH),
                               ACT.Gelu).then_inc(yg_done, 1)
            with act.Fori(0, KC) as m:
                for h in range(2):
                    act.wait_ge(groups, G_E2 + 6 * m + h + 1)
                    act.wait_ge(z_done, 2 * m + h + 1)
                    act.activation(sg2[:, h, :], bank[h][:], ACT.Sigmoid).then_inc(sga_done, 1)
                for h in range(2):
                    act.wait_ge(groups, G_E2 + 6 * m + 4 + h + 1)
                    act.wait_ge(t2_done, 2 * m + h + 1)
                    act.activation(sg2[:, 2 + h, :], bank[4 + h][:], ACT.Sigmoid).then_inc(sgt_done, 1)
            exp_ln_set()
            norm(1, x1, [sq1[:], hx1[:]], rs1, 4, [sq1[:], hx1[:]])
            act.wait_ge(pad_done, 1)
            act.sem_inc(gcopy, 4)
            with act.Fori(0, NF // 2) as f2:
                for p in range(2):
                    f = 2 * f2 + p
                    for h in range(2):
                        act.wait_ge(groups, G_G + 8 * f2 + 4 * p + h + 1)
                        act.activation(gbuf[:, p, 2 + h * HT:2 + (h + 1) * HT], bank[4 * p + h][:], ACT.Copy).then_inc(gcopy, 1)
                    act.wait_ge(cv_done, f + 1)
                    act.activation(cv[:], cv[:], ACT.Gelu).then_inc(gelu_done, 1)
            for mh in range(2):
                for m in range(4):
                    act.wait_ge(out_ready, 8 * mh + 2 * m + 2)
                    act.dma_start(out[4 * mh + m], osb[:, m, :]).then_inc(out_done, 16)
            act.wait_ge(out_done, 16 * KC)

        @block.vector
        def _(dve):
            V = nc.vector
            chain = Chain(dve, dve_c)
            link = chain.link
            TT = V.tensor_tensor

            def hi(n, par, cols=1024, need=None):
                dve.wait_ge(loaded[par], 16 * ring_use(n, par))
                if need is not None:
                    dve.wait_ge(groups, need)
                V.tensor_copy(whi[par][:, 0:cols], raw[par][:, 0:cols]).then_inc(hi_done, 1)

            def ring_use(n, par):
                if isinstance(n, int):
                    return n // 2 + 1
                return (n - par) // 2 + 1

            dve.sem_inc(m_read, 1)
            dve.sem_inc(d_read, 1)
            dve.sem_inc(o_free, 1)
            dve.sem_inc(zb_done, 2)
            dve.sem_inc(t2_done, 2)
            dve.sem_inc(x1_done, 4)
            dve.sem_inc(ff_done, 4)

            dve.wait_ge(lam_in, 16)
            dve.wait_ge(prep_a, 1)
            dve.wait_ge(const_in, 16 * 7)
            lr, li, dt_ = lam_s[:, 0], lam_s[:, 1], pr[:, 0]
            two_pi = 2.0 * np.pi
            c1 = 6.28125
            c2 = float(np.float32(two_pi - c1))
            big = 1.5 * 2.0 ** 23
            link(TT(pr[:, 1], lr, dt_, ALU.mult))
            link(TT(pr[:, 2], li, dt_, ALU.mult))
            link(V.tensor_scalar(pr[:, 3], pr[:, 2], 1.0 / two_pi, big, ALU.mult, ALU.add))
            link(V.tensor_scalar(pr[:, 3], pr[:, 3], -big, None, ALU.add))
            link(V.scalar_tensor_tensor(pr[:, 4], pr[:, 3], -c1, pr[:, 2], ALU.mult, ALU.add))
            link(V.scalar_tensor_tensor(pr[:, 4], pr[:, 3], -c2, pr[:, 4], ALU.mult, ALU.add))
            link(V.tensor_scalar(pr[:, 4], pr[:, 4], 3.1415925, -3.1415925, ALU.min, ALU.max))
            V.tensor_scalar(pr[:, 5], pr[:, 4], 0.5, None, ALU.mult).then_inc(prep_b, 1)
            V.memset(er[:, 0], 1.0)
            link(V.memset(ei[:, 0], 0.0))
            dve.wait_ge(prep_a, 2)
            link(TT(pr[:, 8], pr[:, 7], pr[:, 7], ALU.mult))
            link(V.tensor_scalar(er[:, 1], pr[:, 8], -2.0, 1.0, ALU.mult, ALU.add))
            link(V.tensor_copy(ei[:, 1], pr[:, 6]))

            def cmul(dr, di, ar, ai, br, bi, tmp):
                link(TT(dr, ar, br, ALU.mult))
                link(TT(tmp, ai, bi, ALU.mult))
                link(TT(dr, dr, tmp, ALU.subtract))
                link(TT(di, ai, br, ALU.mult))
                link(TT(tmp, ar, bi, ALU.mult))
                link(TT(di, di, tmp, ALU.add))

            for m in (1, 2, 4):
                b = [x[:, m:m + 1].broadcast_to([P, m, NGROUP]) for x in (er, ei)]
                cmul(er[:, m + 1:2 * m + 1], ei[:, m + 1:2 * m + 1], er[:, 1:m + 1], ei[:, 1:m + 1], *b, pr[:, 8:8 + m])
            V.memset(rtc[:, :, 0], 1.0)
            V.memset(rts[:, :, 0], 0.0)
            V.tensor_copy(rtc[:, :, 1], er[:, 8])
            link(V.tensor_copy(rts[:, :, 1], ei[:, 8]))
            for x in (er, ei):
                link(TT(x[:, 1:], x[:, 1:], mg[:, 1:], ALU.mult))
            V.tensor_copy(mag8[:], mg[:, 8])
            link(TT(pr[:, 8], lr, lr, ALU.mult))
            link(TT(pr[:, 9], li, li, ALU.mult))
            link(TT(pr[:, 8], pr[:, 8], pr[:, 9], ALU.add))
            link(V.reciprocal(pr[:, 8], pr[:, 8]))
            link(V.tensor_scalar(pr[:, 9], er[:, 1], -1.0, None, ALU.add))
            link(TT(pr[:, 10], pr[:, 9], lr, ALU.mult))
            link(TT(pr[:, 11], ei[:, 1], li, ALU.mult))
            link(TT(pr[:, 10], pr[:, 10], pr[:, 11], ALU.add))
            link(TT(pr[:, 10], pr[:, 10], pr[:, 8], ALU.mult))
            link(TT(pr[:, 11], ei[:, 1], lr, ALU.mult))
            link(TT(pr[:, 9], pr[:, 9], li, ALU.mult))
            link(TT(pr[:, 11], pr[:, 11], pr[:, 9], ALU.subtract))
            link(TT(pr[:, 11], pr[:, 11], pr[:, 8], ALU.mult))
            by_n = [x[:].rearrange("p g n -> p n g") for x in (ccr, cci)]
            b = [pr[:, 10 + i].unsqueeze(1).broadcast_to([P, CH, NGROUP]) for i in range(2)]
            flat = rtmp[:].rearrange("p a g k -> p (a g k)")
            cmul(*by_n, er[:, 0:CH], ei[:, 0:CH], *b, flat[:, 0:CH * NGROUP].rearrange("p (n g) -> p n g", n=CH))
            link(V.tensor_scalar(cci[:], cci[:], sgn, None, ALU.mult))
            for dst, src, f in ((g_a, er, gns), (g_b, ei, -1.0), (g_c, ei, sgn), (g_d, er, -1.0)):
                last = V.tensor_scalar(dst[:].rearrange("p g n -> p n g"), src[:], f, None, ALU.mult)
            last.then_inc(prep_b, 1)
            link(V.tensor_scalar(gq[:, 0:1], gq[:, 0:1], DH ** -0.5, None, ALU.mult))

            def norm(which, src, gcol, rs, hxb):
                dve.wait_ge(rs_done, 2 * which + 2)

                def low(k):
                    dve.wait_ge(hhi_done, KC * which + k + 1)
                    TT(hlo[:, k, :], hxb[k % 2], hhi[:, k, :].bitcast(F32), ALU.subtract).then_inc(h_lo, 1)

                for k in range(KC):
                    if k >= 2:
                        low(k - 2)
                        dve.wait_ge(h_lo, KC * which + k - 1)
                    V.scalar_tensor_tensor(hxb[k % 2], src[:, k, :], gcol[:, k:k + 1], rs[:], ALU.mult, ALU.mult).then_inc(hx_done, 1)
                low(KC - 2)
                low(KC - 1)

            norm(0, x0, gm, rs0, [hx[:], utmp[:].rearrange("p j k -> p (j k)")])
            hi(0, 0)

            def rotations():
                m = 1
                while m < NCH:
                    per = min(NGROUP, 1024 // m)
                    for g0 in range(0, NGROUP, per):
                        r = slice(g0, g0 + per)
                        b = [x[:, r, m:m + 1].broadcast_to([P, per, m]) for x in (rtc, rts)]
                        tmp = flat[:, 0:per * m].rearrange("p (g k) -> p g k", k=m)
                        yield lambda r=r, b=b, tmp=tmp, m=m: cmul(rtc[:, r, m + 1:2 * m + 1], rts[:, r, m + 1:2 * m + 1],
                                                                  rtc[:, r, 1:m + 1], rts[:, r, 1:m + 1], *b, tmp)
                    m *= 2

            rot = list(rotations())

            def ublock(hp, n):
                hi(n + 1, 1, need=2 * n if not isinstance(n, int) or n else None)
                for h in range(2):
                    dve.wait_ge(groups, 2 * n + h + 1)
                    if h == 0 and not isinstance(n, int):
                        dve.wait_ge(u_out, 16 * hp)
                    V.tensor_copy(utmp[:].rearrange("p j k -> p k j")[:, h * NCH // 2:(h + 1) * NCH // 2, :],
                                  b_proj[h][:].rearrange("p (k j) -> p k j", j=CH)).then_inc(pev, 1)

            def merge_max(a, ag, hp, h):
                dve.wait_ge(mt_done, 2 * a + h + 1)
                nn, ps, new = natural(run_n[:, :], ag, h), split2(b_nb[:], ag), split2(new_n[:], ag)
                if ag == 0:
                    if h == 0:
                        dve.wait_ge(o_free, hp + 1)
                    V.tensor_copy(nn, ps).then_inc(m_read, 1)
                    return
                dve.wait_ge(merged, 4 * hp + 2 * (ag - 1) + h + 1)
                dve.wait_ge(m_read, 2 * a + h + 1)
                link(TT(new, ps, nn, ALU.min))
                TT(split2(ab[:, 0, :], ag), new, nn, ALU.subtract)
                TT(split2(ab[:, 1, :], ag), new, ps, ALU.subtract).then_inc(m_read, 1)
                dve.wait_ge(m_read, 2 * a + h + 2)
                link(V.tensor_copy(nn, new))

            def merge_sums(a, ag, hp, h):
                nm, nz = natural(num[:, :], ag, h), natural(run_z[:, :], ag, h)
                dve.wait_ge(pv_done, 8 * a + 4 * h + 4)
                dve.wait_ge(dt_done, 2 * a + h + 1)
                if ag == 0:
                    V.tensor_copy(nm, split2(b_o[h][:], ag))
                    V.tensor_copy(nz, split2(b_t[:], ag)).then_inc(d_read, 1)
                    return
                dve.wait_ge(ab_exp, 4 * hp + 2 * (ag - 1) + h + 1)
                TT(t_num[:], b_o[h][:], ab[:, 1, :], ALU.mult)
                TT(t_z[:], b_t[:], ab[:, 1, :], ALU.mult).then_inc(d_read, 1)

            def slot(n, g, b, a, ag, hp):
                par0 = {0: 1, 1: 0, 2: 1}.get(g)
                for j in range(12):
                    if n is not None and j % 4 == 0:
                        k = j // 4
                        hi(b + k + 1, (par0 + k + 1) % 2, need=2 * (b + k))
                    if a is not None and j < 2:
                        dve.wait_ge(vt_done, 2 * a + j + 1)
                        V.tensor_copy(vv[ag][:, 4 * j:4 * j + 4, :].rearrange("p c d -> p (c d)"), b_nb[:]).then_inc(vev_done, 1)
                    if a is not None and j < 8:
                        s0 = keys(ag, j)
                        if j == 0:
                            dve.wait_ge(mask_in[ag], 16 * (hp + 1))
                        dve.wait_ge(s_done, 8 * a + j + 1)
                        dve.sem_inc(waits, 1)
                        dve.wait_ge(rt_out, 32)
                        for x in range(2):
                            last = V.tensor_tensor_reduce(out=sp[:, j % 4, x, s0:], in0=b_s[x][:, 256 * (j % 2) + s0:256 * (j % 2) + 256],
                                                          in1=mask[ag][:, x, s0:], scale=1.0, scalar=-3e38, op0=ALU.add, op1=ALU.max,
                                                          accum_out=mx[:, x:x + 1])
                        link(last)
                        V.tensor_scalar(negm[:, j, :], mx[:], -1.0, None, ALU.mult).then_inc(smx_done, 1)
                    if n is not None and j % 2:
                        gi = j // 2
                        dve.wait_ge(groups, 2 * (b + gi // 2) + gi % 2 + 1)
                        if gi < 4:
                            dve.wait_ge(sq_done, 4 * n + gi + 1)
                        dst = (qn[g], kn[g], vt)[gi // 2]
                        src = b_proj[gi % 2][:].rearrange("p (i r) -> p i r", r=DIL[g])
                        if gi < 4:
                            V.tensor_scalar(by_residue(dst[:, :], g, gi % 2), src, gq[:, gi // 2:gi // 2 + 1], None, ALU.mult).then_inc(pev, 1)
                        else:
                            V.tensor_copy(by_residue(dst[:, :], g, gi % 2), src).then_inc(pev, 1)
                    if a is None and rot:
                        rot.pop(0)()
                    if a is not None and j in (8, 9):
                        h = j - 8
                        dve.wait_ge(exp_done, 8 * a + 4 * h + 4)
                        for i, x in enumerate((negm, den)):
                            last = V.tensor_copy(half(stat[h], i).rearrange("p (s h d) -> p s h d", h=2, d=DH),
                                                 x[:, 4 * h:4 * h + 4, :].unsqueeze(3).broadcast_to([P, 4, 2, DH]))
                        last.then_inc(stat_done, 1)
                    if a is not None and j >= 10:
                        merge_max(a, ag, hp, j - 10)
                        merge_sums(a, ag, hp, j - 10)
                if a is not None and ag == NPAT - 1:
                    dve.wait_ge(merged, 4 * hp + 5)
                    link(V.reciprocal(run_z[:], run_z[:]))
                    TT(num[:], num[:], run_z[:], ALU.mult).then_inc(o_ready, 1)
                if a is None:
                    assert not rot
                    dve.sem_inc(rt_ready, 1)

            stage_a(dve, slot, ublock, lambda hp: chain.enter(hp, 33), chain.leave)

            V.memset(mm_[:], 0.0)
            link(V.memset(zz[:, :, 0], 0.0))
            for q in range(HP):
                dve.wait_ge(o_in[q], 16)
                link(V.tensor_copy(ohi[:, q, :], zb[:, q % 2, :]))
                TT(olo[:, q, :], zb[:, q % 2, :], ohi[:, q, :].bitcast(F32), ALU.subtract).then_inc(osplit, 1)

            def e1(it, first=False):
                b = B_E1 + 4 * it

                def gated(p):
                    for h in range(2):
                        m = 2 * it + p
                        if h == 0 and not first:
                            dve.wait_ge(zb_out[p], 16 * it)
                        dve.wait_ge(sg_done, 2 * m + h + 3)
                        dve.wait_ge(groups, 2 * (b + 2 * p + 1) + h + 1)
                        TT(half(zb[:, p, :], h), bank[2 + h][:], sg[:, h, :], ALU.mult).then_inc(zb_done, 1)

                hi(b + 1, 1, HT, need=2 * b)
                dve.wait_ge(rt_in, 16 * (it + 1))
                for sub in range(2):
                    dve.wait_ge(v_done, 2 * it + sub + 1)
                    r = slice(4 * sub, 4 * sub + 4)
                    v0, v1 = (bank[4 + 2 * sub + i][:].rearrange("p (g k) -> p g k", k=NCH) for i in range(2))
                    TT(ww[:, r], v0, rt[:, 0, r, 1:], ALU.mult)
                    link(TT(wt[:, r], v1, rt[:, 1, r, 1:], ALU.mult))
                    link(TT(ww[:, r], ww[:, r], wt[:, r], ALU.add))
                hi(b + 2, 0, need=2 * (b + 1))
                for gl in range(GB):
                    d = mag8[:].rearrange("p (b g) -> p b g", g=GB)[:, it][:, gl:gl + 1]
                    last = V.tensor_tensor_scan(zz[:, gl, 1:], d.broadcast_to([P, NCH - 1]), ww[:, gl, 0:NCH - 1], 0.0, ALU.mult, ALU.add)
                link(last)
                TT(ww[:], zz[:], rt[:, 0, :, 0:NCH], ALU.mult)
                TT(wt[:], zz[:], rt[:, 1, :, 0:NCH], ALU.mult).then_inc(state_done, 1)
                gated(0)
                hi(b + 3, 1, HT, need=2 * (b + 2))
                hi(b + 4, 0, need=2 * (b + 3))
                gated(1)

            e1(0, first=True)
            with dve.Fori(1, 3) as it:
                chain.enter(it - 1, 5)
                e1(it)
            chain.leave(2)
            e1(3)

            for q in range(HP):
                dve.wait_ge(y_in, 32 * (q + 1))
                V.scalar_tensor_tensor(yu[:, 0, :], yu[:, 1, :], dsk_s[:, q:q + 1], yu[:, 0, :], ALU.mult, ALU.add).then_inc(ydu, 1)
                dve.wait_ge(yg_done, q + 1)
                V.tensor_copy(yhi[:, q, :], zb2[:]).then_inc(ysplit_hi, 1)
            with dve.Fori(0, KC) as m:
                hi(B_E2 + 2 * m + 1, 1, need=G_E2 + 6 * m)
                hi(B_E2 + 2 * m + 2, 0, need=G_E2 + 6 * m + 2)
                for h in range(2):
                    dve.wait_ge(sgt_done, 2 * m + h + 1)
                    dve.wait_ge(z_done, 2 * m + h + 1)
                    TT(t2[:, h, :], bank[2 + h][:], sg2[:, 2 + h, :], ALU.mult).then_inc(t2_done, 1)
            dve.wait_ge(z_done, 2 * KC + 2)
            for k in range(KC):
                link(V.tensor_copy(hhi[:, k, :], zt[:, k, :]))
                TT(hlo[:, k, :], zt[:, k, :], hhi[:, k, :].bitcast(F32), ALU.subtract).then_inc(zs_lo, 1)

            with dve.Fori(0, KC // 2) as m2:
                for p in range(2):
                    hi(B_F + 2 * m2 + p + 1, (p + 1) % 2, need=G_F + 4 * m2 + 2 * p)
                    dve.wait_ge(xr_in[p], 16 * (m2 + 1))
                    for h in range(2):
                        dve.wait_ge(groups, G_F + 4 * m2 + 2 * p + h + 1)
                        TT(half(x1[:].rearrange("p (a b) t -> p b a t", b=2)[:, p, m2, :], h), bank[2 * p + h][:], half(xin[:, p, :], h),
                           ALU.add).then_inc(x1_done, 1)
            norm(1, x1, gf, rs1, [sq1[:], hx1[:]])

            V.memset(gbuf[:, :, 0:2], 0.0).then_inc(pad_done, 1)
            dve.wait_ge(x1_out, 16 * KC)
            with dve.Fori(0, NF // 2) as f2:
                chain.enter(f2, 4)
                for p in range(2):
                    f, n, gr = 2 * f2 + p, B_G + 4 * f2 + 2 * p, G_G + 8 * f2 + 4 * p
                    w = cws[:].rearrange("p (a b) c -> p b a c", b=2)[:, p, f2, :]
                    hi(n + 1, 1, need=gr)
                    hi(n + 2, 0, need=gr + 2)
                    dve.wait_ge(gcopy, 2 * f + 2 + 4)
                    dve.wait_ge(ff_done, 2 * f + 4)
                    link(V.tensor_scalar(cv[:], gbuf[:, p, 2:], w[:, 2:3], w[:, 3:4], ALU.mult, ALU.add))
                    link(V.scalar_tensor_tensor(cv[:], gbuf[:, p, 1:T + 1], w[:, 1:2], cv[:], ALU.mult, ALU.add))
                    V.scalar_tensor_tensor(cv[:], gbuf[:, p, 0:T], w[:, 0:1], cv[:], ALU.mult, ALU.add).then_inc(cv_done, 1)
                    dve.wait_ge(gelu_done, f + 1)
                    for h in range(2):
                        dve.wait_ge(groups, gr + 2 + h + 1)
                        TT(half(ff[:].rearrange("p (a b) t -> p b a t", b=2)[:, p, f2, :], h), half(cv[:], h), bank[4 * p + 2 + h][:],
                           ALU.mult).then_inc(ff_done, 1)
            chain.leave(NF // 2)

            def fsplit(idx, j2, c, first=False):
                if not first:
                    dve.wait_ge((down_used, groups)[c], idx + (0, G_D)[c])
                src = ff[:].rearrange("p (a b) t -> p b a t", b=2)[:, c, j2, :]
                link(V.tensor_copy(fhi[:, c, :], src))
                TT(flo[:, c, :], src, fhi[:, c, :].bitcast(F32), ALU.subtract).then_inc(fs_lo, 1)

            def down(idx, j2, par):
                hi(B_D + idx + 1, par, need=G_D + idx)
                for c in range(2):
                    fsplit(idx + 1, j2, c)

            dve.wait_ge(groups, G_D)
            dve.wait_ge(ff_done, 2 * NF + 4)
            for c in range(2):
                fsplit(0, 0, c, first=True)
            dve.wait_ge(x1r_in, 16 * KC)
            for mh in range(2):
                i0 = 11 * mh
                with dve.Fori(0, 5) as j:
                    chain.enter(j, 4)
                    for q in range(2):
                        down(i0 + 2 * j + q, 2 * j + q + 1, (mh + q + 1) % 2)
                chain.leave(5)
                if mh == 0:
                    down(10, 0, 1)
                for m in range(4):
                    for h in range(2):
                        dve.wait_ge(groups, G_D + i0 + 11)
                        if mh:
                            dve.wait_ge(out_done, 64)
                        TT(half(osb[:, m, :], h), bank[2 * m + h][:], half(x1r[:, 4 * mh + m, :], h), ALU.add).then_inc(out_ready, 1)


def bias_tables():
    i = np.arange(1, NPAT * HEADS + 1, dtype=np.float32)
    slopes = np.exp2(-8.0 * i / (NPAT * HEADS)).astype(np.float32).reshape(HEADS, NPAT).T
    q, k = np.arange(P)[:, None], np.arange(2 * P)[None, :]
    delta = q + P - k
    out = np.empty((NPAT, HEADS, P, 2 * P), np.float32)
    for g, dil in enumerate(DIL):
        valid = (delta >= 0) & (delta <= REACH)
        if T // dil < P:
            n = T // dil
            valid &= (k >= P) & (q // n == (k - P) // n)
        for h in range(HEADS):
            out[g, h] = np.where(valid, -slopes[g, h] * (delta * dil).astype(np.float32), np.float32(NEG))
    return np.ascontiguousarray(out.reshape(NPAT, HP, 2, P, 2 * P).transpose(0, 1, 3, 2, 4))


def blocks(w):
    k, m = w.shape
    return w.reshape(k // P, P, m // P, P).transpose(2, 1, 0, 3).reshape(m // P, P, k)


def kernel(**inputs):
    import concourse.bacc as bacc
    from concourse.bass_utils import run_bass_kernel_spmd

    a = {k: np.asarray(v) for k, v in inputs.items()}
    w_in = a["w_in"][0]
    aw = NPAT * HEADS * DH
    u_b = blocks(w_in[:, :SSM_W])
    qkv = blocks(w_in[:, SSM_W:SSM_W + 3 * aw]).reshape(3, NPAT, HP, P, D)
    ga = blocks(w_in[:, SSM_W + 3 * aw:SSM_W + 3 * aw + D])
    gb = blocks(w_in[:, SSM_W + 3 * aw + D:])
    vg = np.concatenate([blocks(a["glu_w_val"][0]), blocks(a["glu_w_gate"][0])], axis=2)
    fg, fu = blocks(a["ffn_w_gate"][0]), blocks(a["ffn_w_up"][0])
    wd = a["ffn_w_down"][0].reshape(NF // 2, 2, P, 2, HT).transpose(3, 0, 2, 1, 4).reshape(NF, P, 2 * HT)

    stream = [u_b[0], *qkv[:, 0, 0]]
    for hp in range(HP - 1):
        stream += [*qkv[:, 1, hp], *qkv[:, 2, hp], u_b[hp + 1], *qkv[:, 0, hp + 1]]
    stream += [*qkv[:, 1, HP - 1], *qkv[:, 2, HP - 1]]
    stream += [*gb]
    for m in range(KC):
        stream += [ga[m], vg[m]]
    stream += [*blocks(a["w_out"][0])]
    for f in range(NF):
        stream += [fg[f], fu[f]]
    stream += [*wd]

    def cols(v):
        return v.reshape(-1, P).T

    def by_state(x, y):
        return np.concatenate([x.swapaxes(0, 1), y.swapaxes(0, 1)], axis=0)

    lam_re, lam_im, log_dt = a["ssm_lambda_re"][0], a["ssm_lambda_im"][0], a["ssm_log_dt"][0]
    b_re, b_im = a["ssm_b_re"][0], a["ssm_b_im"][0]
    c_re, c_im = (a[x][0].swapaxes(1, 2) for x in ("ssm_c_re", "ssm_c_im"))
    small = np.zeros((P, 3), np.float32)
    small[:NST, 0], small[NST:, 0], small[:NST, 1], small[NST:, 1], small[:, 2] = -1, 1, 1, -1, EPS
    eye = np.eye(P, dtype=np.float32)
    blk = np.kron(np.eye(2, dtype=np.float32), np.ones((DH, DH), np.float32))
    arrays = {
        "xT": a["x"][0].T.reshape(KC, P, T),
        "wblocks": np.stack(stream),
        "wup": blocks(a["w_attn_up"][0]),
        "masks": bias_tables(),
        "consts": np.stack([eye, blk, np.ones((P, P), np.float32)], axis=1),
        "gmix": cols(a["norm_mix_g"][0]),
        "gffn": cols(a["norm_ffn_g"][0]),
        "gqk": np.stack([np.tile(a[x][0], 2) for x in ("q_norm_g", "k_norm_g")], axis=1),
        "lam": np.stack([by_state(lam_re, lam_re), by_state(lam_im, lam_im),
                         np.broadcast_to(log_dt, (P, NGROUP))], axis=1),
        "bmat": np.stack([by_state(b_re, b_im), by_state(b_im, b_re)], axis=1),
        "cmat": np.stack([by_state(c_re, c_im), by_state(c_im, c_re)], axis=1),
        "dsk": cols(a["ssm_d"][0]),
        "cw": np.concatenate([a["ffn_conv_w"][0], a["ffn_conv_b"]], axis=0).T.reshape(NF, P, 4).transpose(1, 0, 2),
        "smallc": small,
    }
    nc = bacc.Bacc("TRN2", target_bir_lowering=False, num_devices=1)
    aps, feed = [], {}
    for name, v in arrays.items():
        v = np.ascontiguousarray(v)
        feed[f"in_{name}"] = v
        aps.append(nc.dram_tensor(f"in_{name}", v.shape, F32, kind="ExternalInput").ap())
    aps.append(nc.dram_tensor("out_t", (KC, P, T), F32, kind="ExternalOutput").ap())
    bass_hybrid_block(nc, *aps)
    r = run_bass_kernel_spmd(nc, [feed], core_ids=[0])
    return np.ascontiguousarray(r.results[0]["out_t"].reshape(D, T).T).reshape(1, T, D)
```

```python
from contextlib import ExitStack

import numpy as np

import concourse.bass as bass
from concourse import mybir

F32 = mybir.dt.float32
F32R = mybir.dt.float32r
ALU = mybir.AluOpType
ACT = mybir.ActivationFunctionType

P = 128
T = 1024
D = 1024
KC = D // P
HT = 512
DH = 64
HEADS = 8
HP = HEADS // 2
DIL = (1, 4, 16)
NPAT = len(DIL)
REACH = 128
NEG = -1e30
EPS = 1e-6
SSM_W = 512
NGROUP = 32
GC = 16
NST = 64
CH = 8
NCH = T // CH
GB = 8
FF = 2816
NF = FF // P
EXP_LN_SET = 6

B_ALOOP, B_AEND, B_U3 = 3, 33, 39
B_E1, B_E2, B_F, B_G, B_D, B_END = 40, 56, 72, 80, 124, 146
GB0_STEPS = (6, 8, 10, 11)
G_E2, G_F, G_G, G_D = 112, 160, 176, 264


class Chain:

    def __init__(self, eng, sem):
        self.eng, self.sem, self.base, self.n = eng, sem, 0, 0

    def link(self, ins):
        self.n += 1
        ins.then_inc(self.sem, 1)
        self.eng.wait_ge(self.sem, self.base + self.n)

    def enter(self, i, per):
        self.start, self.per = self.base + self.n, per
        self.base, self.n = self.start + i * per, 0

    def leave(self, trips):
        assert self.n == self.per, f"steps of one iteration: {self.n}"
        self.base, self.n = self.start + trips * self.per, 0


def bass_hybrid_block(nc, xT, wblocks, wup, masks, consts, gmix, gffn, gqk, lam, bmat, cmat, dsk, cw, smallc, out):
    ctx = ExitStack()
    with ctx:
        def sem(name):
            return ctx.enter_context(nc.semaphore(name))

        def tensors(stack):
            return lambda name, shape, dt=F32: stack.enter_context(nc.sbuf_tensor(name, shape, dt))

        u_scr = nc.dram_tensor("u_scr", [SSM_W, T], F32).ap()
        y_scr = nc.dram_tensor("y_scr", [SSM_W, T], F32).ap()
        o_scr = nc.dram_tensor("o_scr", [HP, P, T], F32).ap()
        zb_scr = nc.dram_tensor("zb_scr", [KC, P, T], F32).ap()
        x1_scr = nc.dram_tensor("x1_scr", [KC, P, T], F32).ap()
        rt_scr = nc.dram_tensor("rt_scr", [P, 2, NGROUP, NCH + 1], F32).ap()

        sb = tensors(ctx)
        cst_s = sb("cst_s", [P, 3, P])
        ident, blk_ones, ones = cst_s[:, 0], cst_s[:, 1], cst_s[:, 2]
        small = sb("small", [P, 3])
        sgn, gns, epsc = small[:, 0:1], small[:, 1:2], small[:, 2:3]
        gm = sb("gm", [P, KC])
        gf = sb("gf", [P, KC])
        gq = sb("gq", [P, 2])
        dsk_s = sb("dsk_s", [P, HP])
        cws = sb("cws", [P, NF, 4])
        raw = [sb(f"raw{i}", [P, 1024]) for i in range(2)]
        whi = [sb(f"whi{i}", [P, 1024], F32R) for i in range(2)]
        wlo = [sb(f"wlo{i}", [P, 1024], F32R) for i in range(2)]
        ccr = sb("ccr", [P, NGROUP, CH])
        cci = sb("cci", [P, NGROUP, CH])
        g_a = sb("g_a", [P, NGROUP, CH + 1])
        g_b = sb("g_b", [P, NGROUP, CH + 1])
        g_c = sb("g_c", [P, NGROUP, CH + 1])
        g_d = sb("g_d", [P, NGROUP, CH + 1])
        mag8 = sb("mag8", [P, NGROUP])
        h_stack = ExitStack()
        sb = tensors(h_stack)
        hhi = sb("hhi", [P, KC, T], F32R)
        hlo = sb("hlo", [P, KC, T], F32R)

        with ExitStack() as s:
            sb = tensors(s)
            qkv_t = [[sb(f"{x}{g}", [P, T]) for x in ("qn", "kn", "vv")] for g in range(2)]
            sp = sb("sp", [P, 4, 2, 256])
            ptr = sb("ptr", [P, 2, HT])
            vt = sb("vt", [P, T])
            qkv_t.append([sb(f"{x}2", [P, T]) for x in ("qn", "kn", "vv")])
            qn, kn = ([t[i] for t in qkv_t] for i in range(2))
            vv = [t[2][:].rearrange("p (c d) -> p c d", d=P) for t in qkv_t]
            run_n = sb("run_n", [P, T])
            run_z = sb("run_z", [P, T])
            num = sb("num", [P, T])
            ab_h0 = sb("ab_h0", [P, 2, HT])
            t_num = sb("t_num", [P, 2, HT])
            t_z = sb("t_z", [P, HT])
        with ExitStack() as s:
            sb = tensors(s)
            x0 = sb("x0", [P, KC, T])
            rs0 = sb("rs0", [P, T])
            sb("over_vt", [P, T])
            rt0 = sb("rt0", [P, 2, NGROUP, NCH + 1])
            rtc, rts = rt0[:, 0], rt0[:, 1]
        with ExitStack() as s:
            sb = tensors(s)
            sb("over_a", [P, 9 * T + T + 2 * T + 4 * T + 4 * HT + HT])
            mask = [sb(f"mask{g}", [P, 2, 256]) for g in range(NPAT)]
            sq = sb("sq", [P, 2, HT])
            rn = sb("rn", [P, 2, HT])
            mx = sb("mx", [P, 2])
            negm = sb("negm", [P, 8, 2])
            den = sb("den", [P, 8, 2])
            utmp = sb("utmp", [P, CH, NCH])
            rtmp = sb("rtmp", [P, 2, GB, NCH // 2])
            hx = sb("hx", [P, T])
            with ExitStack() as s_prep:
                sb = tensors(s_prep)
                lam_s = sb("lam_s", [P, 3, NGROUP])
                pr = sb("pr", [P, 12, NGROUP])
                er = sb("er", [P, 9, NGROUP])
                ei = sb("ei", [P, 9, NGROUP])
                mg = sb("mg", [P, 9, NGROUP])
            with ExitStack() as s_ab:
                ab_h1 = tensors(s_ab)("ab_h1", [P, 2, HT])
            ab = (ab_h0, ab_h1)
        with ExitStack() as s:
            sb = tensors(s)
            tb = sb("tb", [P, GB, CH, GC])
            gp = sb("gp", [P, GB, CH, GC])
            gg = sb("gg", [P, GB, CH + 1, GC])
            ttmp = sb("ttmp", [P, GB, CH + 1, GC])
            b_in = sb("b_in", [P, 2, GB, GC])
            c_in = sb("c_in", [P, 2, GB, GC])
            uu = sb("uu", [P, GB, NCH])
            sb("pad_uu", [P, 2 * P])
            ohi = sb("ohi", [P, HP, T], F32R)
            olo = sb("olo", [P, HP, T], F32R)
            zz = sb("zz", [P, GB, NCH])
            ww = sb("ww", [P, GB, NCH])
            wt = sb("wt", [P, GB, NCH])
            mm_ = sb("mm_", [P, GB, P])
            zb = [sb(f"zb{p}", [P, T]) for p in (1, 0)][::-1]
            o_st = sb("o_st", [P, 2, T])
            w1 = sb("w1", [P, GB, P])
            w1p = sb("w1p", [P, GB, P])
            rt = sb("rt", [P, 2, GB, NCH + 1])
            kt = sb("kt", [GC, GB, P])
        with ExitStack() as s:
            sb = tensors(s)
            yhi = sb("yhi", [P, HP, T], F32R)
            gt = sb("gt", [P, 2, T])
            zt = sb("zt", [P, KC, T])
            ylo = sb("ylo", [P, HP, T], F32R)
            zb2 = sb("zb2", [P, T])
            sb("over_zb_sg", [P, 3 * T])
            sg2 = sb("sg2", [P, 4, HT])
            t2 = sb("t2", [P, 2, HT])
        with ExitStack() as s:
            sb = tensors(s)
            uraw = sb("uraw", [P, HP, T])
            sb("over_gt_zt", [P, 10 * T])
            yraw = sb("yraw", [P, HP, T])
        with ExitStack() as s:
            sb = tensors(s)
            sqb1 = sb("sqb1", [P, 2, T])
            ssq = sb("ssq", [P, T])
            rs1 = sb("rs1", [P, T])
            hx1 = sb("hx1", [P, T])
            sb("pad_hx1", [P, T])
            x1 = sb("x1", [P, KC, T])
            sb("over_ylo_zb2", [P, 5 * T])
            xin = sb("xin", [P, 2, T])
        with ExitStack() as s:
            sb = tensors(s)
            ff = sb("ff", [P, NF, T])
            gbuf = sb("gbuf", [P, 2, T + 2])
            cv = sb("cv", [P, T])
        h_stack.close()
        with ExitStack() as s:
            sb = tensors(s)
            fhi = sb("fhi", [P, 2, T], F32R)
            flo = sb("flo", [P, 2, T], F32R)
            x1r = sb("x1r", [P, KC, T])
            osb = sb("osb", [P, KC // 2, T])

        stat = [hx[:], rtmp[:].rearrange("p a g k -> p (a g k)")]

        bank = [ctx.enter_context(nc.psum_tensor(f"bank{i}", [P, HT], F32)) for i in range(8)]
        b_proj, b_nb, b_s, b_t, b_o = bank[0:2], bank[2], bank[3:5], bank[5], bank[6:8]

        loaded = [sem(f"loaded{i}") for i in range(2)]
        hi_done, lo_done = sem("hi_done"), sem("lo_done")
        groups = sem("groups")
        const_in, cst_in, small_in, lam_in, x_in = sem("const_in"), sem("cst_in"), sem("small_in"), sem("lam_in"), [sem(f"x_in{i}") for i in range(KC)]
        dve_c, act_c, pool_c, waits = sem("dve_c"), sem("act_c"), sem("pool_c"), sem("waits")
        xsq_done, rs_done, ssx_done = sem("xsq_done"), sem("rs_done"), sem("ssx_done")
        prep_a, prep_b = sem("prep_a"), sem("prep_b")
        rt_ready, rot_ready, rot_done = sem("rt_ready"), sem("rot_ready"), sem("rot_done")
        pev, sq_done, ss_done, rn_done, nrm_done = (sem(x) for x in ("pev", "sq_done", "ss_done", "rn_done", "nrm_done"))
        vt_done, vev_done = sem("vt_done"), sem("vev_done")
        s_done, smx_done, exp_done, t_done, tev, pv_done = (sem(x) for x in ("s_done", "smx_done", "exp_done", "t_done", "tev", "pv_done"))
        mask_in = [sem(f"mask_in{g}") for g in range(NPAT)]
        mt_done, dt_done, m_read, d_read, ab_exp, merged, stat_done = (
            sem(x) for x in ("mt_done", "dt_done", "m_read", "d_read", "ab_exp", "merged", "stat_done"))
        z_sum, rz_done = sem("z_sum"), sem("rz_done")
        o_ready, o_out, u_out = sem("o_ready"), sem("o_out"), sem("u_out")

        o_in, osplit = [sem(f"o_in{i}") for i in range(HP - 1)], sem("osplit")
        sg_done, zb_done = sem("sg_done"), sem("zb_done")
        zb_out = [sem(f"zb_out{i}") for i in range(2)]
        bc_in, tb_done, gt_done, gp_done = sem("bc_in"), sem("tb_done"), sem("gt_done"), sem("gp_done")
        tr_done, w1_done, kt_done, m_in = (sem(x) for x in ("tr_done", "w1_done", "kt_done", "m_in"))
        u_in, rt_in, v_done, state_done, y_done, y_ev, y_out = (
            sem(x) for x in ("u_in", "rt_in", "v_done", "state_done", "y_done", "y_ev", "y_out"))
        mm_zero = sem("mm_zero")
        y_in, ydu, yg_done, ysplit_hi, ysplit = [sem(f"y_in{i}") for i in range(HP)], sem("ydu"), sem("yg_done"), sem("ysplit_hi"), sem("ysplit")
        sga_done, sgt_done, zb_in, z_done = (sem(x) for x in ("sga_done", "sgt_done", "zb_in", "z_done"))
        zs_hi, zs_lo = sem("zs_hi"), sem("zs_lo")
        t2_done, kt_ev, ln_done = sem("t2_done"), sem("kt_ev"), sem("ln_done")
        xr_in = [sem(f"xr_in{i}") for i in range(2)]
        x1_done, x1_out = sem("x1_done"), sem("x1_out")
        hx_done, hhi_done, h_lo = sem("hx_done"), sem("hhi_done"), sem("h_lo")
        gcopy, cv_done, gelu_done, ff_done, pad_done = (sem(x) for x in ("gcopy", "cv_done", "gelu_done", "ff_done", "pad_done"))
        acc_done = sem("acc_done")
        fs_lo, down_used, tile_done = sem("fs_lo"), sem("down_used"), sem("tile_done")
        x1r_in, out_ready, out_done = sem("x1r_in"), sem("out_ready"), sem("out_done")

        def half(ap, h):
            return ap[:, h * HT:(h + 1) * HT]

        def by_residue(ap, g, h):
            dil = DIL[g]
            n = T // dil
            return ap.rearrange("p (r i) -> p i r", r=dil)[:, h * n // 2:(h + 1) * n // 2, :]

        def natural(ap, g, h):
            dil = DIL[g]
            v = ap.rearrange("p (i r) -> p r i", r=dil)
            return half(ap, h).rearrange("p (r i) -> p r i", r=1) if dil == 1 else v[:, h * dil // 2:(h + 1) * dil // 2, :]

        def split2(ap, g):
            dil = DIL[g]
            return ap.rearrange("p (r i) -> p r i", r=1 if dil == 1 else dil // 2)

        def keys(g, s):
            return 0 if (g == 0 and s > 0) or (g == 1 and s % 2) else P

        def stage_a(eng, slot, ublock, enter=None, leave=None):
            slot(0, 0, 0, None, None, None)
            with eng.Fori(0, HP - 1) as hp:
                if enter:
                    enter(hp)
                b = B_ALOOP + 10 * hp
                slot(3 * hp + 1, 1, b, 3 * hp, 0, hp)
                slot(3 * hp + 2, 2, b + 3, 3 * hp + 1, 1, hp)
                ublock(hp, b + 6)
                slot(3 * hp + 3, 0, b + 7, 3 * hp + 2, 2, hp)
            if leave:
                leave(HP - 1)
            last = 3 * (HP - 1)
            slot(last + 1, 1, B_AEND, last, 0, HP - 1)
            slot(last + 2, 2, B_AEND + 3, last + 1, 1, HP - 1)
            slot(None, None, None, last + 2, 2, HP - 1)

        def rotations(link, tt, g0, tmp_):
            ops, m, r = [], 1, slice(g0, g0 + NGROUP // 2)
            while m < NCH:
                br, bi = (x[:, r, m:m + 1].broadcast_to([P, NGROUP // 2, m]) for x in (rtc, rts))
                (dr, ar), (di, ai) = ((x[:, r, m + 1:2 * m + 1], x[:, r, 1:m + 1]) for x in (rtc, rts))
                tmp = tmp_[:, 0:NGROUP // 2 * m].rearrange("p (g k) -> p g k", k=m)
                for args in ((dr, ar, br, ALU.mult), (tmp, ai, bi, ALU.mult), (dr, dr, tmp, ALU.subtract),
                             (di, ai, br, ALU.mult), (tmp, ar, bi, ALU.mult), (di, di, tmp, ALU.add)):
                    ops.append(lambda args=args: link(tt(*args)))
                m *= 2
            return ops

        block = ctx.enter_context(nc.Block())

        @block.sync
        def _(sp_):
            def load(n, src, par, cols=1024, first=False):
                if not first:
                    sp_.wait_ge(lo_done, n - 1)
                sp_.dma_start(raw[par][:, 0:cols], src).then_inc(loaded[par], 16)

            sp_.dma_start(lam_s[:], lam).then_inc(lam_in, 16)
            sp_.dma_start(small[:], smallc).then_inc(small_in, 16)
            for k in range(KC):
                sp_.dma_start(x0[:, k, :], xT[k]).then_inc(x_in[k], 16)
            for n in range(2):
                load(n, wblocks[n], n, first=True)
            for g in range(NPAT):
                sp_.dma_start(mask[g][:], masks[g, 0]).then_inc(mask_in[g], 16)
            load(2, wblocks[2], 0)

            def save_u(hp):
                sp_.wait_ge(pev, 20 * hp + 20)
                sp_.dma_start(u_scr.rearrange("(q c) t -> q c t", c=P)[hp],
                              utmp[:].rearrange("p j k -> p (j k)")).then_inc(u_out, 16)

            def load_bc(it):
                sp_.dma_start(b_in[:], bmat.rearrange("p a (b g) c -> b p a g c", g=GB)[it]).then_inc(bc_in, 16)
                sp_.dma_start(c_in[:], cmat.rearrange("p a (b g) c -> b p a g c", g=GB)[it]).then_inc(bc_in, 16)

            def load_uu(it):
                for n in range(CH):
                    sp_.dma_start(uu[GC * n:GC * (n + 1)],
                                  u_scr.rearrange("(b g c) (j k) -> j b c g k", g=GB, c=GC, k=NCH)[CH - 1 - n, it]).then_inc(u_in, 16)

            def load_rt(it):
                sp_.dma_start(rt[:], rt_scr.rearrange("p a (b g) k -> b p a g k", g=GB)[it]).then_inc(rt_in, 16)

            with sp_.Fori(0, HP - 1) as hp:
                for b in range(10):
                    load(B_ALOOP + 10 * hp + b, wblocks[B_ALOOP + 10 * hp + b], (b + 1) % 2)
                save_u(hp)
            for n in range(B_AEND, B_E1 + 1):
                load(n, wblocks[n], n % 2)
            sp_.wait_ge(pv_done, 8 * 11)
            load_bc(0)
            load(B_E1 + 1, wblocks[B_E1 + 1], 1)
            save_u(HP - 1)
            sp_.wait_ge(u_out, 16 * HP + 1)
            load_uu(0)
            load(B_E1 + 2, wup[0], 0, HT)
            sp_.wait_ge(nrm_done, 4 * 12)
            sp_.wait_ge(o_out, 16 * HP)
            for q in range(HP - 1):
                if q == 2:
                    sp_.wait_ge(osplit, 1)
                sp_.dma_start(o_st[:, q % 2, :], o_scr[q]).then_inc(o_in[q], 16)
            load(B_E1 + 3, wup[1], 1, HT)
            sp_.wait_ge(o_ready, 2 * HP)
            load_rt(0)

            def e1(it, first=False, last=False):
                if not first:
                    sp_.wait_ge(y_done, 2 * it)
                    load_uu(it)
                    sp_.wait_ge(state_done, it)
                    load_rt(it)
                b = B_E1 + 4 * it
                if not last:
                    sp_.wait_ge(gp_done, it + 1)
                    load_bc(it + 1)
                if not first:
                    load(b + 2, wblocks[B_E1 + 2 * it + 1], 0)
                    load(b + 3, wup[2 * it + 1], 1, HT)
                if not last:
                    load(b + 4, wblocks[B_E1 + 2 * it + 2], 0)
                    load(b + 5, wup[2 * it + 2], 1, HT)
                else:
                    load(b + 4, wblocks[48], 0)
                    load(b + 5, wblocks[49], 1)
                for p in range(2):
                    if last and p == 1:
                        sp_.wait_ge(y_done, 2 * HP)
                        for q in range(HP):
                            load_y(q)
                    sp_.wait_ge(zb_done, 4 * it + 2 * p + 4)
                    sp_.dma_start(zb_scr[2 * it + p], zb[p][:]).then_inc(zb_out[p], 16)

            def load_y(q):
                sp_.wait_ge(y_out, 16 * CH * (q + 1))
                sp_.dma_start(uraw[:, q, :], u_scr.rearrange("(q c) t -> q c t", c=P)[q]).then_inc(y_in[q], 16)
                sp_.dma_start(yraw[:, q, :], y_scr.rearrange("(q c) t -> q c t", c=P)[q]).then_inc(y_in[q], 16)

            e1(0, first=True)
            with sp_.Fori(1, 3) as it:
                e1(it)
            e1(3, last=True)
            for p in range(2):
                sp_.wait_ge(zb_out[p], 64)
            with sp_.Fori(0, KC) as m:
                sp_.wait_ge(z_done, 2 * m + 2)
                sp_.dma_start(zb2[:], zb_scr[m]).then_inc(zb_in, 16)
                load(B_E2 + 2 * m + 2, wblocks[50 + 2 * m], 0)
                load(B_E2 + 2 * m + 3, wblocks[51 + 2 * m], 1)
            for p in range(2):
                sp_.dma_start(xin[:, p, :], xT[p]).then_inc(xr_in[p], 16)
            for m in range(2, KC):
                load(B_F + m, wblocks[64 + m], m % 2)
                sp_.wait_ge(x1_done, 2 * (m - 1) + 4)
                sp_.dma_start(xin[:, m % 2, :], xT[m]).then_inc(xr_in[m % 2], 16)
            load(B_G, wblocks[72], 0)
            load(B_G + 1, wblocks[73], 1)
            for m in range(KC):
                sp_.wait_ge(x1_done, 2 * (m + 1) + 4)
                sp_.dma_start(x1_scr[m], x1[:, m, :]).then_inc(x1_out, 16)
            sp_.wait_ge(x1_out, 16 * KC)
            with sp_.Fori(0, NF // 2) as f2:
                for b in range(4):
                    load(B_G + 2 + 4 * f2 + b, wblocks[74 + 4 * f2 + b], b % 2)
            sp_.wait_ge(groups, G_D)
            for m in range(KC):
                sp_.dma_start(x1r[:, m, :], x1_scr[m]).then_inc(x1r_in, 16)
            with sp_.Fori(0, 10) as j:
                load(B_D + 2 + 2 * j, wblocks[118 + 2 * j], 0)
                load(B_D + 3 + 2 * j, wblocks[119 + 2 * j], 1)

        @block.gpsimd
        def _(pool):
            chain = Chain(pool, pool_c)
            for dst, src in ((gm, gmix), (gq, gqk), (gf, gffn), (dsk_s, dsk), (cws, cw)):
                pool.dma_start(dst[:], src).then_inc(const_in, 16)

            def lo(n, par, cols=1024):
                pool.wait_ge(hi_done, n + 1)
                pool.tensor_tensor(wlo[par][:, 0:cols], raw[par][:, 0:cols], whi[par][:, 0:cols].bitcast(F32),
                                   ALU.subtract).then_inc(lo_done, 1)

            pool.wait_ge(rot_ready, 1)
            for n, op in enumerate(rotations(chain.link, pool.tensor_tensor, NGROUP // 2, vt[:])):
                if n in (30, 36):
                    lo(n // 6 - 5, n // 6 - 5)
                op()
            pool.sem_inc(rot_done, 1)

            def ublock(hp, n):
                lo(n + 1, 0)

            def tb_table(it):
                pool.wait_ge(bc_in, 32 * (it + 1))
                cr, ci = (x.rearrange("p (b g) n -> p b g n", g=GB)[:, it].unsqueeze(3).broadcast_to([P, GB, CH, GC])
                          for x in (ccr[:], cci[:]))
                b0, b1 = (b_in[:, i].unsqueeze(2).broadcast_to([P, GB, CH, GC]) for i in range(2))
                chain.link(pool.tensor_tensor(tb[:], cr, b0, ALU.mult))
                chain.link(pool.tensor_tensor(ttmp[:, :, 0:CH], ci, b1, ALU.mult))
                chain.link(pool.tensor_tensor(tb[:], tb[:], ttmp[:, :, 0:CH], ALU.add))
                pool.sem_inc(tb_done, 1)

            def c_table(it, dst, x, y, lo_, n, done):
                cr, ci = (q.rearrange("p (b g) n -> p b g n", g=GB)[:, it][:, :, lo_:].unsqueeze(3).broadcast_to([P, GB, n, GC])
                          for q in (x[:], y[:]))
                c0, c1 = (c_in[:, i].unsqueeze(2).broadcast_to([P, GB, n, GC]) for i in range(2))
                chain.link(pool.tensor_tensor(dst[:], cr, c0, ALU.mult))
                chain.link(pool.tensor_tensor(ttmp[:, :, 0:n], ci, c1, ALU.mult))
                chain.link(pool.tensor_tensor(dst[:], dst[:], ttmp[:, :, 0:n], ALU.add))
                pool.sem_inc(done, 1)

            def g_table(it):
                c_table(it, gg, g_a, g_b, 0, CH + 1, gt_done)

            def gp_table(it):
                c_table(it, gp, g_c, g_d, 1, CH, gp_done)
            def slot(n, g, b, a, ag, hp):
                par0 = {0: 0, 1: 1, 2: 0}.get(g)
                for j in range(12):
                    if n is not None and j % 4 == 0:
                        k = j // 4 + 1
                        if a is not None or j:
                            lo(b + k, (par0 + k) % 2)
                    if n is not None and j in (3, 5, 7, 9):
                        gi = (j - 3) // 2
                        pool.wait_ge(rn_done, 4 * n + gi + 1)
                        pool.wait_ge(pev, 2 * (b + gi // 2) + gi % 2 + 1)
                        dst = by_residue((qn if gi < 2 else kn)[g][:, :], g, gi % 2)
                        src = rn[:, gi % 2, :].rearrange("p (i r) -> p i r", r=DIL[g])
                        pool.tensor_tensor(dst, dst, src, ALU.mult).then_inc(nrm_done, 1)
                    if a is not None and ag > 0 and j in (10, 11):
                        h = j - 10
                        nm = natural(num[:, :], ag, h)
                        pool.wait_ge(ab_exp, hpc(hp, ag) + h + 1)
                        chain.link(pool.tensor_tensor(nm, nm, split2(ab[h][:, 0, :], ag), ALU.mult))
                        pool.wait_ge(d_read, 2 * a + h + 2)
                        pool.tensor_tensor(nm, nm, split2(t_num[:, h, :], ag), ALU.add).then_inc(merged, 1)
                        if ag == NPAT - 1:
                            pool.wait_ge(merged, hpc(hp, ag) + h + 3)
                            pool.wait_ge(rz_done, 2 * hp + h + 1)
                            pool.tensor_tensor(nm, nm, natural(run_z[:, :], ag, h), ALU.mult).then_inc(o_ready, 1)
                    if n is None and j == 0:
                        lo(B_E1, 0)
                        pool.wait_ge(prep_b, 2)
                        tb_table(0)
                    if n is None and j == 4:
                        lo(B_E1 + 1, 1)
                        g_table(0)
                        gp_table(0)
                if a is None:
                    pool.wait_ge(rt_ready, 1)
                    pool.dma_start(rt_scr, rt0[:]).then_inc(o_out, 16)
                if n is not None and ag == NPAT - 1:
                    pool.wait_ge(o_ready, 2 * hp + 2)
                    pool.dma_start(o_scr[hp], num[:]).then_inc(o_out, 16)

            def hpc(hp, ag):
                return 4 * hp + 2 * (ag - 1)

            pool.sem_inc(merged, 2)
            stage_a(pool, slot, ublock, lambda hp: chain.enter(hp, 4), chain.leave)

            def e1(it, last=False):
                b = B_E1 + 4 * it
                lo(b + 1, 1, HT)
                lo(b + 2, 0)
                if not last:
                    pool.wait_ge(kt_done, it + 1)
                    tb_table(it + 1)
                lo(b + 3, 1, HT)
                lo(b + 4, 0)
                if not last:
                    pool.wait_ge(y_done, 2 * it + 2)
                    g_table(it + 1)
                    gp_table(it + 1)

            lo(B_E1 + 2, 0, HT)
            lo(B_E1 + 3, 1, HT)
            pool.wait_ge(kt_done, 1)
            tb_table(1)
            lo(B_E1 + 4, 0)
            pool.wait_ge(y_done, 2)
            g_table(1)
            gp_table(1)
            with pool.Fori(1, 3) as it:
                chain.enter(it - 1, 9)
                e1(it)
            chain.leave(2)
            e1(3, last=True)
            pool.sem_inc(z_done, 2)
            with pool.Fori(0, KC) as m:
                chain.enter(m, 2)
                lo(B_E2 + 2 * m + 1, 1)
                lo(B_E2 + 2 * m + 2, 0)
                pool.wait_ge(zb_in, 16 * (m + 1))
                for h in range(2):
                    pool.wait_ge(sga_done, 2 * m + h + 3)
                    pool.wait_ge(t2_done, 2 * m + h + 3)
                    chain.link(pool.tensor_tensor(t2[:, h, :], t2[:, h, :], sg2[:, h, :], ALU.mult))
                    pool.tensor_tensor(half(zt[:, m, :], h), t2[:, h, :], half(zb2[:], h), ALU.add).then_inc(z_done, 1)
            chain.leave(KC)

            def add_squares(k, p):
                pool.wait_ge(xsq_done, KC + 2 * k + 2)
                pool.wait_ge(acc_done, k)
                pool.tensor_tensor(ssq[:], ssq[:], sqb1[:, p, :], ALU.add).then_inc(acc_done, 1)

            pool.sem_inc(acc_done, 1)
            lo(B_F + 1, 1)
            lo(B_F + 2, 0)
            with pool.Fori(1, KC // 2) as m2:
                lo(B_F + 2 * m2 + 1, 1)
                add_squares(2 * m2 - 1, 1)
                lo(B_F + 2 * m2 + 2, 0)
                add_squares(2 * m2, 0)
            with pool.Fori(0, NF // 2) as f2:
                for b in range(4):
                    lo(B_G + 4 * f2 + b + 1, (b + 1) % 2)
            with pool.Fori(0, 10) as j:
                lo(B_D + 2 * j + 1, 1)
                lo(B_D + 2 * j + 2, 0)
            lo(B_END - 1, 1)

        @block.tensor
        def _(pe):
            def mm3(ps, par, w0, k_list, hi, lo_, h, start, stop):
                for k in k_list:
                    c = w0(k)
                    a, b, x, y = whi[par][:, c:c + P], wlo[par][:, c:c + P], half(hi[:, k, :], h), half(lo_[:, k, :], h)
                    nc.tensor.matmul(ps, a, x, start=start and k == k_list[0], stop=False)
                    nc.tensor.matmul(ps, a, y, start=False, stop=False)
                    last = nc.tensor.matmul(ps, b, x, start=False, stop=stop and k == k_list[-1])
                return last

            def cols(k):
                return k * P

            def ready(n):
                pe.wait_ge(lo_done, n + 1)

            def by_chunk(split, base, outs):
                for k in range(KC):
                    pe.wait_ge(split, base + k + 1)
                    for bk, par, h in outs:
                        last = mm3(bk[:], par, cols, [k], hhi, hlo, h, k == 0, k == KC - 1)
                        if k == KC - 1:
                            last.then_inc(groups, 1)

            pe.wait_ge(cst_in, 16)
            for k in range(KC):
                pe.wait_ge(xsq_done, k + 1)
                sqk = (sq, rn)[k % 2]
                for h in range(2):
                    m_ = nc.tensor.matmul(bank[h][:], ones, sqk[:, h, :], start=k == 0, stop=k == KC - 1)
                m_.then_inc(ssx_done, 1)

            def ublock(hp, n):
                ready(n)
                for h in range(2):
                    pe.wait_ge(pev, 2 * n + h - 1)
                    mm3(b_proj[h][:], 1, cols, range(KC), hhi, hlo, h, True, True).then_inc(groups, 1)

            def quarter(n, par, i):
                h, part = i // 2, i % 2
                if part == 0:
                    if h == 0:
                        ready(n)
                    pe.wait_ge(pev, 2 * n + h - 1)
                last = mm3(b_proj[h][:], par, cols, range(4 * part, 4 * part + 4), hhi, hlo, h, part == 0, part == 1)
                if part == 1:
                    last.then_inc(groups, 1)

            def slot(n, g, b, a, ag, hp):
                par0 = {0: 0, 1: 1, 2: 0}.get(g)
                for j in range(12):
                    if n is None and j < 4:
                        quarter(B_U3, 1, j)
                    if n is None and j in GB0_STEPS:
                        quarter(B_E1, 0, GB0_STEPS.index(j))
                    if a is None and j == 0:
                        ready(0)
                        pe.wait_ge(rs_done, 2)
                        by_chunk(h_lo, 0, [(b_proj[h], 0, h) for h in range(2)])
                    if n is not None and (a is not None or j > 3):
                        blk, h, part = j // 4, j // 2 % 2, j % 2
                        if part == 0:
                            if h == 0:
                                ready(b + blk)
                            pe.wait_ge(pev, 2 * (b + blk) + h - 1)
                            if blk:
                                pe.wait_ge(sq_done, 4 * n + 2 * (blk - 1) + h + 1)
                        last = mm3(b_proj[h][:], (par0 + blk) % 2, cols, range(4 * part, 4 * part + 4), hhi, hlo, h,
                                   part == 0, part == 1)
                        if part == 1:
                            last.then_inc(groups, 1)
                    if a is not None:
                        if j in (0, 1):
                            if j == 0:
                                pe.wait_ge(m_read, 2 * a + 1)
                                pe.wait_ge(ln_done, 4 * a + 4)
                                pe.wait_ge(pev, vgroups(ag, hp))
                            else:
                                pe.wait_ge(vev_done, 2 * a + 1)
                            for c in range(4):
                                last = nc.tensor.transpose(b_nb[:, c * P:(c + 1) * P], vt[:, (4 * j + c) * P:(4 * j + c + 1) * P], ident)
                            last.then_inc(vt_done, 1)
                        if j < 8:
                            s0 = keys(ag, j)
                            if j == 0:
                                pe.wait_ge(nrm_done, 4 * a + 4)
                            else:
                                pe.wait_ge(smx_done, 8 * a + j)
                            for x in range(2):
                                r = slice(DH * x, DH * (x + 1))
                                last = nc.tensor.matmul(b_s[x][:, 256 * (j % 2) + s0:256 * (j % 2) + 256], qn[ag][r, j * P:(j + 1) * P],
                                                        kn[ag][r, (j - 1) * P + s0:(j + 1) * P], start=True, stop=True)
                            last.then_inc(s_done, 1)
                        if 2 <= j < 10:
                            s_ = j - 2
                            pe.wait_ge(exp_done, 8 * a + s_ + 1)
                            if s_ == 0:
                                pe.wait_ge(d_read, 2 * a + 1)
                            else:
                                pe.wait_ge(tev, 8 * a + s_)
                            for x in range(2):
                                for kb in range(keys(ag, s_) // P, 2):
                                    c = (2 * x + kb) * P
                                    last = nc.tensor.transpose(b_t[:, c:c + P], sp[:, s_ % 4, x, kb * P:(kb + 1) * P], ident)
                            last.then_inc(t_done, 1)
                        if 3 <= j < 11:
                            s_ = j - 3
                            if s_ == 0:
                                pe.wait_ge(vev_done, 2 * a + 2)
                            pe.wait_ge(tev, 8 * a + s_ + 1)
                            k0 = keys(ag, s_) // P
                            for x in range(2):
                                r = slice(DH * x, DH * (x + 1))
                                for kb in range(k0, 2):
                                    c = (2 * x + kb) * P
                                    last = nc.tensor.matmul(b_o[s_ // 4][r, (s_ % 4) * P:(s_ % 4 + 1) * P], vv[ag][:, s_ - 1 + kb, r],
                                                            ptr[:, s_ % 2, c:c + P], start=kb == k0, stop=kb == 1)
                            last.then_inc(pv_done, 1)
                    if n is not None and j in (2, 4, 6, 8):
                        gi = (j - 2) // 2
                        pe.wait_ge(sq_done, 4 * n + gi + 1)
                        if gi == 0:
                            if a is not None:
                                pe.wait_ge(vev_done, 2 * a + 2)
                        else:
                            pe.wait_ge(ln_done, 4 * n + gi)
                        nc.tensor.matmul(b_nb[:], blk_ones, sq[:, gi % 2, :], start=True, stop=True).then_inc(ss_done, 1)
                    if a is not None and j in (9, 11):
                        h = (j - 9) // 2
                        pe.wait_ge(stat_done, 2 * a + h + 1)
                        if h:
                            pe.wait_ge(m_read, 2 * a + 2)
                        elif n is not None:
                            pe.wait_ge(ln_done, 4 * n + 4)
                        for s_ in range(4):
                            last = nc.tensor.transpose(b_nb[:, s_ * P:(s_ + 1) * P], stat[h][:, s_ * P:(s_ + 1) * P], ident)
                        last.then_inc(mt_done, 1)
                    if a is not None and j in (10, 11):
                        h = j - 10
                        if h:
                            pe.wait_ge(d_read, 2 * a + 2)
                        else:
                            pe.wait_ge(tev, 8 * a + 8)
                        for s_ in range(4):
                            last = nc.tensor.transpose(b_t[:, s_ * P:(s_ + 1) * P], stat[h][:, HT + s_ * P:HT + (s_ + 1) * P], ident)
                        last.then_inc(dt_done, 1)

            def vgroups(ag, hp):
                return 20 * hp + {0: 6, 1: 12, 2: 18}[ag]

            stage_a(pe, slot, ublock)

            def tables(it, first=False):
                pe.wait_ge(tb_done, it + 1)
                if not first:
                    pe.wait_ge(y_ev, 2 * it)
                for sub in range(2):
                    for q4 in range(4):
                        gl = 4 * sub + q4
                        last = nc.tensor.transpose(bank[4 + sub][:, q4 * P:(q4 + 1) * P], tb[:, gl].rearrange("p n c -> p (n c)"), ident)
                    last.then_inc(tr_done, 1)

            def taps(it):
                pe.wait_ge(gt_done, it + 1)
                for sub in range(2):
                    for q4 in range(4):
                        gl = 4 * sub + q4
                        last = nc.tensor.matmul(bank[6 + sub][0:GC, q4 * P:(q4 + 1) * P], tb[:, gl, 0, :],
                                                gg[:, gl, 0:CH].rearrange("p n c -> p (n c)"), start=True, stop=True)
                last.then_inc(kt_done, 1)

            def chunk_inputs(it):
                pe.wait_ge(w1_done, 2 * it + 2)
                pe.wait_ge(kt_ev, it + 1)
                pe.wait_ge(u_in, 16 * CH * (it + 1))
                for sub in range(2):
                    for q4 in range(4):
                        gl = 4 * sub + q4
                        nc.tensor.matmul(bank[4 + 2 * sub][:, q4 * P:(q4 + 1) * P], w1[:, gl], uu[:, gl], start=True, stop=True)
                        last = nc.tensor.matmul(bank[5 + 2 * sub][:, q4 * P:(q4 + 1) * P], w1p[:, gl], uu[:, gl], start=True, stop=True)
                    last.then_inc(v_done, 1)

            def chunk_outputs(it):
                pe.wait_ge(state_done, it + 1)
                pe.wait_ge(m_in, 16 * CH * (it + 1))
                pe.wait_ge(gp_done, it + 1)
                for sub in range(2):
                    for q4 in range(4):
                        gl = 4 * sub + q4
                        ps = bank[4 + sub][:, q4 * P:(q4 + 1) * P]
                        nc.tensor.matmul(ps, mm_[:, gl], uu[:, gl], start=True, stop=False)
                        nc.tensor.matmul(ps, gg[:, gl, 1:].rearrange("p n c -> p (n c)"), ww[:, gl], start=False, stop=False)
                        last = nc.tensor.matmul(ps, gp[:, gl].rearrange("p n c -> p (n c)"), wt[:, gl], start=False, stop=True)
                    last.then_inc(y_done, 1)

            def gate(m, par, h, part, bk=None):
                if part == 0 and not bk:
                    pe.wait_ge(sg_done, 2 * m + h + 1)
                last = mm3((bk or bank[h])[:], par, cols, range(4 * part, 4 * part + 4), hhi, hlo, h, part == 0, part == 1)
                if part:
                    last.then_inc(groups, 1)

            def up(m, par, h):
                pe.wait_ge(zb_done, 2 * m + h + 1)
                mm3(bank[2 + h][:], par, cols, range(HP), ohi, olo, h, True, True).then_inc(groups, 1)

            def e1(it):
                for p in range(2):
                    m, n = 2 * it + p, B_E1 + 4 * it + 2 * p
                    ready(n)
                    gate(m, 0, 0, 0)
                    if p == 0:
                        tables(it)
                    gate(m, 0, 0, 1)
                    gate(m, 0, 1, 0)
                    if p == 0:
                        taps(it)
                    if p == 1:
                        chunk_outputs(it)
                    gate(m, 0, 1, 1)
                    if p == 0:
                        chunk_inputs(it)
                    ready(n + 1)
                    up(m, 1, 0)
                    up(m, 1, 1)

            ready(B_E1 + 1)
            pe.wait_ge(smx_done, 8 * 12)
            gate(1, 1, 0, 0, bank[3])
            gate(1, 1, 0, 1, bank[3])
            pe.wait_ge(d_read, 2 * 12 + 1)
            tables(0, first=True)
            taps(0)
            gate(1, 1, 1, 0)
            gate(1, 1, 1, 1)
            chunk_inputs(0)
            pe.wait_ge(osplit, HP)
            for p in range(2):
                ready(B_E1 + 2 + p)
                up(p, p, 0)
                if p == 0:
                    pe.wait_ge(sg_done, 2 * 1 + 3)
                up(p, p, 1)
            chunk_outputs(0)
            with pe.Fori(1, 3) as it:
                e1(it)
            e1(3)

            def e2(m, first=False):
                n = B_E2 + 2 * m
                ready(n)
                for h in range(2):
                    pe.wait_ge(sga_done, 2 * m + h + 1)
                    mm3(bank[h][:], 0, cols, range(KC), hhi, hlo, h, True, True).then_inc(groups, 1)
                ready(n + 1)
                for w in range(2):
                    for h in range(2):
                        pe.wait_ge(t2_done, 2 * m + h + 1)
                        if first and w == h == 0:
                            pe.wait_ge(zb_done, 2 * KC + 2)
                        for k in range(HP):
                            if first and w == h == 0:
                                pe.wait_ge(ysplit, k + 1)
                            last = mm3(bank[2 + 2 * w + h][:], 1, lambda k: (4 * w + k) * P, [k], yhi, ylo, h, k == 0, k == HP - 1)
                        last.then_inc(groups, 1)

            e2(0, first=True)
            with pe.Fori(1, KC) as m:
                e2(m)

            def out_block(m2, p):
                ready(B_F + 2 * m2 + p)
                for h in range(2):
                    pe.wait_ge(x1_done, 4 * m2 + 2 * p + h + 1)
                    mm3(bank[2 * p + h][:], p, cols, range(KC), hhi, hlo, h, True, True).then_inc(groups, 1)

            ready(B_F)
            by_chunk(zs_lo, 0, [(bank[h], 0, h) for h in range(2)])
            out_block(0, 1)
            with pe.Fori(1, KC // 2) as m2:
                for p in range(2):
                    out_block(m2, p)

            pe.wait_ge(acc_done, KC - 1)
            for h in range(2):
                nc.tensor.matmul(bank[4 + h][:], ones, half(ssq[:], h), start=True, stop=False)
            for h in range(2):
                pe.wait_ge(xsq_done, KC + 2 * KC - 1 + h)
                nc.tensor.matmul(bank[4 + h][:], ones, half(sqb1[:, 1, :], h), start=False, stop=True).then_inc(ssx_done, 1)

            def ffn_pair(f2, p):
                n = B_G + 4 * f2 + 2 * p
                for w in range(2):
                    ready(n + w)
                    for h in range(2):
                        pe.wait_ge((gcopy, ff_done)[w], 4 * f2 + 2 * p + h + 1)
                        mm3(bank[4 * p + 2 * w + h][:], w, cols, range(KC), hhi, hlo, h, True, True).then_inc(groups, 1)

            ready(B_G + 1)
            by_chunk(h_lo, KC, [(bank[2 * w + h], w, h) for w in range(2) for h in range(2)])
            ffn_pair(0, 1)
            with pe.Fori(1, NF // 2) as f2:
                for p in range(2):
                    ffn_pair(f2, p)

            def down(idx, par, start=False, stop=False, free=None):
                ready(B_D + idx)
                for c in range(2):
                    pe.wait_ge(fs_lo, 2 * idx + c + 1)
                    for m in range(4):
                        for h in range(2):
                            if free and c == 0:
                                pe.wait_ge(out_ready, 2 * m + h + 1)
                            last = mm3(bank[2 * m + h][:], par, lambda k: c * HT + m * P, [c], fhi, flo, h,
                                       start and c == 0, stop and c == 1)
                        if stop and c == 1 and m < 3:
                            last.then_inc(tile_done, 1)
                    last.then_inc((down_used, groups)[c], 1)

            pe.wait_ge(ff_done, 2 * NF + 4)
            for mh in range(2):
                i0 = 11 * mh
                down(i0, mh, start=True, free=mh)
                with pe.Fori(0, 4) as j:
                    for q in range(2):
                        down(i0 + 1 + 2 * j + q, (mh + 1 + q) % 2)
                down(i0 + 9, (mh + 1) % 2)
                down(i0 + 10, mh, stop=True)

        @block.scalar
        def _(act):
            def exp_ln_set():
                act.add_instruction(mybir.InstLoadActFuncSet(
                    name=nc.get_next_instruction_name(), engine=act.engine, act_func_set_id=EXP_LN_SET))

            chain = Chain(act, act_c)
            act.dma_start(cst_s[:], consts).then_inc(cst_in, 16)
            exp_ln_set()

            def square_x(k):
                act.wait_ge(x_in[k], 16)
                if k >= 2:
                    act.wait_ge(ssx_done, k - 1)
                act.activation((sq, rn)[k % 2][:].rearrange("p a t -> p (a t)"), x0[:, k, :], ACT.Square).then_inc(xsq_done, 1)

            act.wait_ge(lam_in, 16)
            act.activation(pr[:, 0], lam_s[:, 2], ACT.Exp).then_inc(prep_a, 1)
            square_x(0)
            square_x(1)
            act.wait_ge(prep_b, 1)
            for n in range(1, 9):
                act.activation(mg[:, n], pr[:, 1], ACT.Exp, scale=float(n))
            act.activation(pr[:, 6], pr[:, 4], ACT.Sin)
            act.activation(pr[:, 7], pr[:, 5], ACT.Sin).then_inc(prep_a, 1)
            exp_ln_set()

            def norm(which, rs, b0, hxb):
                for h in range(2):
                    act.wait_ge(ssx_done, KC + (1 + h if which else 0))
                    chain.link(act.activation(half(rs[:], h), bank[b0 + h][:], ACT.Ln, scale=1.0 / D, bias=epsc))
                    act.activation(half(rs[:], h), half(rs[:], h), ACT.Exp, scale=-0.5).then_inc(rs_done, 1)
                for k in range(KC):
                    act.wait_ge(hx_done, KC * which + k + 1)
                    act.activation(hhi[:, k, :], hxb[k % 2], ACT.Copy).then_inc(hhi_done, 1)

            act.wait_ge(small_in, 16)
            for k in range(2, KC):
                square_x(k)
            norm(0, rs0, 0, [hx[:], utmp[:].rearrange("p j k -> p (j k)")])

            def ublock(hp, n):
                pass

            def reciprocal_z(hp, ag, h):
                nz = natural(run_z[:, :], ag, h)
                act.wait_ge(z_sum, 2 * hp + h + 1)
                chain.link(act.activation(nz, nz, ACT.Ln))
                act.activation(nz, nz, ACT.Exp, scale=-1.0).then_inc(rz_done, 1)

            def slot(n, g, b, a, ag, hp):
                for j in range(12):
                    if n is not None and j % 2 and j < 8:
                        gi = j // 2
                        act.wait_ge(groups, 2 * (b + gi // 2) + gi % 2 + 1)
                        if gi >= 2:
                            act.wait_ge(ss_done, 4 * n + gi - 1)
                        act.activation(sq[:, gi % 2, :], b_proj[gi % 2][:], ACT.Square).then_inc(sq_done, 1)
                    if a is not None and 2 <= j < 10:
                        s_ = j - 2
                        act.wait_ge(t_done, 8 * a + s_ + 1)
                        src, dst = (x.rearrange("p (h q) -> p h q", h=2)[:, :, keys(ag, s_):] for x in (b_t[:], ptr[:, s_ % 2, :]))
                        act.activation(dst, src, ACT.Copy).then_inc(tev, 1)
                    if n is not None and j in (2, 4, 6, 8):
                        gi = (j - 2) // 2
                        act.wait_ge(ss_done, 4 * n + gi + 1)
                        if not isinstance(n, int) or n or gi >= 2:
                            act.wait_ge(nrm_done, 4 * n + gi - 1)
                        act.activation(rn[:, gi % 2, :], b_nb[:], ACT.Ln, scale=1.0 / DH, bias=epsc).then_inc(ln_done, 1)
                        act.wait_ge(ln_done, 4 * n + gi + 1)
                        act.activation(rn[:, gi % 2, :], rn[:, gi % 2, :], ACT.Exp, scale=-0.5).then_inc(rn_done, 1)
                    if a is not None and j < 8:
                        act.wait_ge(smx_done, 8 * a + j + 1)
                        s0 = keys(ag, j)
                        for x in range(2):
                            last = act.activation(sp[:, j % 4, x, s0:], sp[:, j % 4, x, s0:], ACT.Exp,
                                                  bias=negm[:, j, x:x + 1], accum_out=den[:, j, x:x + 1])
                        last.then_inc(exp_done, 1)
                    if a is not None and j == 8 and not isinstance(hp, int):
                        act.dma_start(mask[ag][:], masks[ag, hp + 1]).then_inc(mask_in[ag], 16)
                    if a is not None and ag and j >= 10:
                        h = j - 10
                        act.wait_ge(m_read, 2 * a + h + 2)
                        act.activation(ab[h][:], ab[h][:], ACT.Exp).then_inc(ab_exp, 1)
                        if ag == NPAT - 1 and (n is not None or h == 0):
                            reciprocal_z(hp, ag, h)

            stage_a(act, slot, ublock, lambda hp: chain.enter(hp, 2), chain.leave)

            def sigmoid_b(it, p, h, block, bk=None):
                act.wait_ge(groups, 2 * block + h + 1)
                if not isinstance(it, int) or it:
                    act.wait_ge(zb_out[p], 16 * it)
                act.activation(half(zb[p][:], h), (bk or bank[h])[:], ACT.Sigmoid).then_inc(sg_done, 1)

            def e1(it, first=False, last=False):
                if first:
                    act.wait_ge(u_out, 16 * HP + 1)
                else:
                    act.wait_ge(y_out, 16 * CH * it)
                for sub in range(2):
                    act.wait_ge(tr_done, 2 * it + sub + 1)
                    v = bank[4 + sub][:].rearrange("p (g s) -> p g s", s=P)
                    r = slice(4 * sub, 4 * sub + 4)
                    act.activation(w1[:, r], v, ACT.Copy)
                    act.activation(w1p[:, r, 0:NST], v[:, :, NST:], ACT.Copy)
                    act.activation(w1p[:, r, NST:], v[:, :, 0:NST], ACT.Copy, scale=-1.0).then_inc(w1_done, 1)
                if not first:
                    sigmoid_b(it, 0, 0, B_E1 + 4 * it)
                act.wait_ge(kt_done, it + 1)
                act.activation(kt[:, 0:4], bank[6][0:GC, :].rearrange("p (g s) -> p g s", s=P), ACT.Copy)
                act.activation(kt[:, 4:8], bank[7][0:GC, :].rearrange("p (g s) -> p g s", s=P), ACT.Copy).then_inc(kt_ev, 1)
                if first:
                    for h in range(2):
                        sigmoid_b(0, 1, h, B_E1 + 1, bank[3] if h == 0 else None)
                else:
                    sigmoid_b(it, 0, 1, B_E1 + 4 * it)
                act.wait_ge(kt_ev, it + 1)
                if first:
                    act.wait_ge(mm_zero, 1)
                for n in range(CH):
                    j = CH - 1 - n
                    act.dma_start(mm_[GC * n:GC * (n + 1), :, GC * j:], kt[:, :, 0:P - GC * j]).then_inc(m_in, 16)
                for h in range(2):
                    if not first:
                        sigmoid_b(it, 1, h, B_E1 + 4 * it + 2)
                    if last:
                        act.wait_ge(sg_done, 2 * KC + h + 1)
                        act.sem_inc(sga_done, 1)
                    if h:
                        continue
                    for sub in range(2):
                        act.wait_ge(y_done, 2 * it + sub + 1)
                        act.activation(w1p[:, 4 * sub:4 * sub + 4], bank[4 + sub][:].rearrange("p (g s) -> p g s", s=P),
                                       ACT.Copy).then_inc(y_ev, 1)
                    act.wait_ge(y_ev, 2 * it + 2)
                    for i in range(CH):
                        act.dma_start(y_scr.rearrange("(b g c) (i k) -> i b c g k", g=GB, c=GC, k=NCH)[i, it],
                                      w1p[GC * i:GC * (i + 1)]).then_inc(y_out, 16)

            act.sem_inc(sg_done, 2)
            for h in range(2):
                sigmoid_b(0, 0, h, B_E1)
            exp_ln_set()
            reciprocal_z(HP - 1, NPAT - 1, 1)
            e1(0, first=True)
            with act.Fori(1, 3) as it:
                e1(it)
            e1(3, last=True)
            for q in range(HP):
                act.wait_ge(ydu, q + 1)
                if q >= 2:
                    act.wait_ge(ysplit, q - 1)
                act.activation(gt[:, q % 2, :].rearrange("p (k i) -> p i k", i=CH), yraw[:, q, :].rearrange("p (i k) -> p i k", i=CH),
                               ACT.Gelu).then_inc(yg_done, 1)
                act.wait_ge(yg_done, q + 1)
                act.activation(yhi[:, q, :], gt[:, q % 2, :], ACT.Copy).then_inc(ysplit_hi, 1)

            def z_hi(k):
                act.wait_ge(z_done, 2 * k + 4)
                act.activation(hhi[:, k, :], zt[:, k, :], ACT.Copy).then_inc(zs_hi, 1)

            def e2(m, last=False):
                for h in range(2):
                    act.wait_ge(groups, G_E2 + 6 * m + h + 1)
                    act.wait_ge(z_done, 2 * m + h + 1)
                    act.activation(sg2[:, h, :], bank[h][:], ACT.Sigmoid).then_inc(sga_done, 1)
                if last:
                    for k in range(KC - 1):
                        z_hi(k)
                for h in range(2):
                    act.wait_ge(groups, G_E2 + 6 * m + 4 + h + 1)
                    act.wait_ge(t2_done, 2 * m + h + 1)
                    act.activation(sg2[:, 2 + h, :], bank[4 + h][:], ACT.Sigmoid).then_inc(sgt_done, 1)

            with act.Fori(0, KC - 1) as m:
                e2(m)
            e2(KC - 1, last=True)
            z_hi(KC - 1)
            exp_ln_set()
            for k in range(KC):
                for h in range(2):
                    act.wait_ge(x1_done, 2 * k + h + 1 + 4)
                    if k >= 3 and h == 0:
                        act.wait_ge(acc_done, k - 1)
                    act.activation(half((sqb1[:, k % 2, :] if k else ssq[:]), h), half(x1[:, k, :], h), ACT.Square).then_inc(xsq_done, 1)
            norm(1, rs1, 4, [sqb1[:, 0, :], hx1[:]])
            act.wait_ge(pad_done, 1)
            act.sem_inc(gcopy, 4)
            with act.Fori(0, NF // 2) as f2:
                for p in range(2):
                    f = 2 * f2 + p
                    for h in range(2):
                        act.wait_ge(groups, G_G + 8 * f2 + 4 * p + h + 1)
                        act.activation(gbuf[:, p, 2 + h * HT:2 + (h + 1) * HT], bank[4 * p + h][:], ACT.Copy).then_inc(gcopy, 1)
                    act.wait_ge(cv_done, f + 1)
                    act.activation(cv[:], cv[:], ACT.Gelu).then_inc(gelu_done, 1)
            for mh in range(2):
                for m in range(4):
                    act.wait_ge(out_ready, 8 * mh + 2 * m + 2)
                    act.dma_start(out[4 * mh + m], osb[:, m, :]).then_inc(out_done, 16)
            act.wait_ge(out_done, 16 * KC)

        @block.vector
        def _(dve):
            V = nc.vector
            chain = Chain(dve, dve_c)
            link = chain.link
            TT = V.tensor_tensor

            def hi(n, par, cols=1024, need=None):
                dve.wait_ge(loaded[par], 16 * ring_use(n, par))
                if need is not None:
                    dve.wait_ge(groups, need)
                V.tensor_copy(whi[par][:, 0:cols], raw[par][:, 0:cols]).then_inc(hi_done, 1)

            def ring_use(n, par):
                if isinstance(n, int):
                    return n // 2 + 1
                return (n - par) // 2 + 1

            dve.sem_inc(m_read, 1)
            dve.sem_inc(d_read, 1)
            dve.sem_inc(u_out, 1)
            dve.sem_inc(zb_done, 2)
            dve.sem_inc(t2_done, 2)
            dve.sem_inc(x1_done, 4)
            dve.sem_inc(ff_done, 4)

            dve.wait_ge(lam_in, 16)
            dve.wait_ge(prep_a, 1)
            dve.wait_ge(small_in, 16)
            lr, li, dt_ = lam_s[:, 0], lam_s[:, 1], pr[:, 0]
            two_pi = 2.0 * np.pi
            c1 = 6.28125
            c2 = float(np.float32(two_pi - c1))
            big = 1.5 * 2.0 ** 23
            link(TT(pr[:, 1], lr, dt_, ALU.mult))
            link(TT(pr[:, 2], li, dt_, ALU.mult))
            link(V.tensor_scalar(pr[:, 3], pr[:, 2], 1.0 / two_pi, big, ALU.mult, ALU.add))
            link(V.tensor_scalar(pr[:, 3], pr[:, 3], -big, None, ALU.add))
            link(V.scalar_tensor_tensor(pr[:, 4], pr[:, 3], -c1, pr[:, 2], ALU.mult, ALU.add))
            link(V.scalar_tensor_tensor(pr[:, 4], pr[:, 3], -c2, pr[:, 4], ALU.mult, ALU.add))
            link(V.tensor_scalar(pr[:, 4], pr[:, 4], 3.1415925, -3.1415925, ALU.min, ALU.max))
            V.tensor_scalar(pr[:, 5], pr[:, 4], 0.5, None, ALU.mult).then_inc(prep_b, 1)
            V.memset(er[:, 0], 1.0)
            link(V.memset(ei[:, 0], 0.0))
            dve.wait_ge(prep_a, 2)
            link(TT(pr[:, 8], pr[:, 7], pr[:, 7], ALU.mult))
            link(V.tensor_scalar(er[:, 1], pr[:, 8], -2.0, 1.0, ALU.mult, ALU.add))
            link(V.tensor_copy(ei[:, 1], pr[:, 6]))

            def cmul(dr, di, ar, ai, br, bi, tmp):
                link(TT(dr, ar, br, ALU.mult))
                link(TT(tmp, ai, bi, ALU.mult))
                link(TT(dr, dr, tmp, ALU.subtract))
                link(TT(di, ai, br, ALU.mult))
                link(TT(tmp, ar, bi, ALU.mult))
                link(TT(di, di, tmp, ALU.add))

            for m in (1, 2, 4):
                b = [x[:, m:m + 1].broadcast_to([P, m, NGROUP]) for x in (er, ei)]
                cmul(er[:, m + 1:2 * m + 1], ei[:, m + 1:2 * m + 1], er[:, 1:m + 1], ei[:, 1:m + 1], *b, pr[:, 8:8 + m])
            V.memset(rtc[:, :, 0], 1.0)
            V.memset(rts[:, :, 0], 0.0)
            V.tensor_copy(rtc[:, :, 1], er[:, 8])
            link(V.tensor_copy(rts[:, :, 1], ei[:, 8]))
            dve.sem_inc(rot_ready, 1)
            for x in (er, ei):
                link(TT(x[:, 1:], x[:, 1:], mg[:, 1:], ALU.mult))
            V.tensor_copy(mag8[:], mg[:, 8])
            link(TT(pr[:, 8], lr, lr, ALU.mult))
            link(TT(pr[:, 9], li, li, ALU.mult))
            link(TT(pr[:, 8], pr[:, 8], pr[:, 9], ALU.add))
            link(V.reciprocal(pr[:, 8], pr[:, 8]))
            link(V.tensor_scalar(pr[:, 9], er[:, 1], -1.0, None, ALU.add))
            link(TT(pr[:, 10], pr[:, 9], lr, ALU.mult))
            link(TT(pr[:, 11], ei[:, 1], li, ALU.mult))
            link(TT(pr[:, 10], pr[:, 10], pr[:, 11], ALU.add))
            link(TT(pr[:, 10], pr[:, 10], pr[:, 8], ALU.mult))
            link(TT(pr[:, 11], ei[:, 1], lr, ALU.mult))
            link(TT(pr[:, 9], pr[:, 9], li, ALU.mult))
            link(TT(pr[:, 11], pr[:, 11], pr[:, 9], ALU.subtract))
            link(TT(pr[:, 11], pr[:, 11], pr[:, 8], ALU.mult))
            by_n = [x[:].rearrange("p g n -> p n g") for x in (ccr, cci)]
            b = [pr[:, 10 + i].unsqueeze(1).broadcast_to([P, CH, NGROUP]) for i in range(2)]
            flat = rtmp[:].rearrange("p a g k -> p (a g k)")
            cmul(*by_n, er[:, 0:CH], ei[:, 0:CH], *b, flat[:, 0:CH * NGROUP].rearrange("p (n g) -> p n g", n=CH))
            link(V.tensor_scalar(cci[:], cci[:], sgn, None, ALU.mult))
            for dst, src, f in ((g_a, er, gns), (g_b, ei, -1.0), (g_c, ei, sgn), (g_d, er, -1.0)):
                last = V.tensor_scalar(dst[:].rearrange("p g n -> p n g"), src[:], f, None, ALU.mult)
            last.then_inc(prep_b, 1)
            dve.wait_ge(const_in, 16 * 5)
            link(V.tensor_scalar(gq[:, 0:1], gq[:, 0:1], DH ** -0.5, None, ALU.mult))

            def norm(which, src, gcol, rs, hxb):
                dve.wait_ge(rs_done, 2 * which + 2)

                def low(k):
                    dve.wait_ge(hhi_done, KC * which + k + 1)
                    TT(hlo[:, k, :], hxb[k % 2], hhi[:, k, :].bitcast(F32), ALU.subtract).then_inc(h_lo, 1)

                for k in range(KC):
                    if k >= 2:
                        low(k - 2)
                        dve.wait_ge(h_lo, KC * which + k - 1)
                    V.scalar_tensor_tensor(hxb[k % 2], src[:, k, :], gcol[:, k:k + 1], rs[:], ALU.mult, ALU.mult).then_inc(hx_done, 1)
                low(KC - 2)
                low(KC - 1)

            hi(0, 0)
            hi(1, 1)
            norm(0, x0, gm, rs0, [hx[:], utmp[:].rearrange("p j k -> p (j k)")])

            rot = rotations(link, TT, 0, flat)

            def evict_u(hp, n, h):
                dve.wait_ge(groups, 2 * n + h + 1)
                if h == 0:
                    dve.wait_ge(u_out, 16 * hp + 1)
                V.tensor_copy(utmp[:].rearrange("p j k -> p k j")[:, h * NCH // 2:(h + 1) * NCH // 2, :],
                              b_proj[h][:].rearrange("p (k j) -> p k j", j=CH)).then_inc(pev, 1)

            def ublock(hp, n):
                hi(n + 1, 0, need=2 * n)
                for h in range(2):
                    evict_u(hp, n, h)

            def merge_max(a, ag, hp, h):
                dve.wait_ge(mt_done, 2 * a + h + 1)
                nn, ps, new = natural(run_n[:, :], ag, h), split2(b_nb[:], ag), split2(t_z[:], ag)
                if ag == 0:
                    if h == 0:
                        dve.wait_ge(o_out, 16 * (hp + 1))
                    V.tensor_copy(nn, ps).then_inc(m_read, 1)
                    return
                dve.wait_ge(merged, 4 * hp + 2 * (ag - 1) + h + 1)
                dve.wait_ge(m_read, 2 * a + h + 1)
                link(TT(new, ps, nn, ALU.min))
                TT(split2(ab[h][:, 0, :], ag), new, nn, ALU.subtract)
                TT(split2(ab[h][:, 1, :], ag), new, ps, ALU.subtract).then_inc(m_read, 1)
                dve.wait_ge(m_read, 2 * a + h + 2)
                link(V.tensor_copy(nn, new))

            def merge_sums(a, ag, hp, h):
                nm, nz = natural(num[:, :], ag, h), natural(run_z[:, :], ag, h)
                dve.wait_ge(pv_done, 8 * a + 4 * h + 4)
                dve.wait_ge(dt_done, 2 * a + h + 1)
                if ag == 0:
                    V.tensor_copy(nm, split2(b_o[h][:], ag))
                    V.tensor_copy(nz, split2(b_t[:], ag)).then_inc(d_read, 1)
                    return
                dve.wait_ge(ab_exp, 4 * hp + 2 * (ag - 1) + h + 1)
                TT(t_num[:, h, :], b_o[h][:], ab[h][:, 1, :], ALU.mult)
                TT(t_z[:], b_t[:], ab[h][:, 1, :], ALU.mult).then_inc(d_read, 1)
                link(TT(nz, nz, split2(ab[h][:, 0, :], ag), ALU.mult))
                dve.wait_ge(d_read, 2 * a + h + 2)
                link(TT(nz, nz, split2(t_z[:], ag), ALU.add))
                if ag == NPAT - 1:
                    dve.sem_inc(z_sum, 1)

            def slot(n, g, b, a, ag, hp):
                par0 = {0: 0, 1: 1, 2: 0}.get(g)
                for j in range(12):
                    if n is not None and j % 4 == 0:
                        k = j // 4
                        if a is not None or k:
                            hi(b + k + 1, (par0 + k + 1) % 2, need=2 * (b + k))
                    if a is not None and j < 2:
                        dve.wait_ge(vt_done, 2 * a + j + 1)
                        V.tensor_copy(vv[ag][:, 4 * j:4 * j + 4, :].rearrange("p c d -> p (c d)"), b_nb[:]).then_inc(vev_done, 1)
                    if a is not None and j < 8:
                        s0 = keys(ag, j)
                        if j == 0:
                            dve.wait_ge(mask_in[ag], 16 * (hp + 1))
                        dve.wait_ge(s_done, 8 * a + j + 1)
                        dve.sem_inc(waits, 1)
                        dve.wait_ge(h_lo, KC)
                        for x in range(2):
                            last = V.tensor_tensor_reduce(out=sp[:, j % 4, x, s0:], in0=b_s[x][:, 256 * (j % 2) + s0:256 * (j % 2) + 256],
                                                          in1=mask[ag][:, x, s0:], scale=1.0, scalar=-3e38, op0=ALU.add, op1=ALU.max,
                                                          accum_out=mx[:, x:x + 1])
                        link(last)
                        V.tensor_scalar(negm[:, j, :], mx[:], -1.0, None, ALU.mult).then_inc(smx_done, 1)
                    if n is not None and j % 2:
                        gi = j // 2
                        dve.wait_ge(groups, 2 * (b + gi // 2) + gi % 2 + 1)
                        if gi < 4:
                            dve.wait_ge(sq_done, 4 * n + gi + 1)
                        dst = (qn[g], kn[g], vt)[gi // 2]
                        src = b_proj[gi % 2][:].rearrange("p (i r) -> p i r", r=DIL[g])
                        if gi == 4 and a is None:
                            dve.wait_ge(rot_done, 1)
                        if gi < 4:
                            V.tensor_scalar(by_residue(dst[:, :], g, gi % 2), src, gq[:, gi // 2:gi // 2 + 1], None, ALU.mult).then_inc(pev, 1)
                        else:
                            V.tensor_copy(by_residue(dst[:, :], g, gi % 2), src).then_inc(pev, 1)
                    if n is None and j == 0:
                        hi(B_E1, 0, need=2 * B_U3)
                    if n is None and j in (2, 4):
                        evict_u(hp, B_U3, j // 2 - 1)
                    if n is None and j == 4:
                        hi(B_E1 + 1, 1, need=2 * B_E1)
                    if a is None:
                        for _ in range(7 if j < 4 else 2):
                            if rot:
                                rot.pop(0)()
                    if a is not None and j in (8, 9):
                        h = j - 8
                        dve.wait_ge(exp_done, 8 * a + 4 * h + 4)
                        for i, x in enumerate((negm, den)):
                            last = V.tensor_copy(half(stat[h], i).rearrange("p (s h d) -> p s h d", h=2, d=DH),
                                                 x[:, 4 * h:4 * h + 4, :].unsqueeze(3).broadcast_to([P, 4, 2, DH]))
                        last.then_inc(stat_done, 1)
                    if a is not None and j >= 10:
                        merge_max(a, ag, hp, j - 10)
                        merge_sums(a, ag, hp, j - 10)
                if n is None:
                    for q in range(HP - 1):
                        dve.wait_ge(o_in[q], 16)
                        link(V.tensor_copy(ohi[:, q, :], o_st[:, q % 2, :]))
                        TT(olo[:, q, :], o_st[:, q % 2, :], ohi[:, q, :].bitcast(F32), ALU.subtract).then_inc(osplit, 1)
                    hi(B_E1 + 2, 0, HT, need=2 * (B_E1 + 1))
                if a is None:
                    assert not rot
                    dve.sem_inc(rt_ready, 1)

            stage_a(dve, slot, ublock, lambda hp: chain.enter(hp, 40), chain.leave)

            dve.wait_ge(o_ready, 2 * HP)
            link(V.tensor_copy(ohi[:, HP - 1, :], num[:]))
            TT(olo[:, HP - 1, :], num[:], ohi[:, HP - 1, :].bitcast(F32), ALU.subtract).then_inc(osplit, 1)
            dve.wait_ge(osplit, HP)
            V.memset(mm_[:], 0.0).then_inc(mm_zero, 1)
            link(V.memset(zz[:, :, 0], 0.0))

            def gated(it, p, block):
                for h in range(2):
                    m = 2 * it + p
                    dve.wait_ge(sg_done, 2 * m + h + 3)
                    dve.wait_ge(groups, 2 * block + h + 1)
                    TT(half(zb[p][:], h), bank[2 + h][:], half(zb[p][:], h), ALU.mult).then_inc(zb_done, 1)

            def rotate(it):
                dve.wait_ge(rt_in, 16 * (it + 1))
                for sub in range(2):
                    dve.wait_ge(v_done, 2 * it + sub + 1)
                    r = slice(4 * sub, 4 * sub + 4)
                    v0, v1 = (bank[4 + 2 * sub + i][:].rearrange("p (g k) -> p g k", k=NCH) for i in range(2))
                    TT(ww[:, r], v0, rt[:, 0, r, 1:], ALU.mult)
                    link(TT(wt[:, r], v1, rt[:, 1, r, 1:], ALU.mult))
                    link(TT(ww[:, r], ww[:, r], wt[:, r], ALU.add))

            def scan(it):
                for gl in range(GB):
                    d = mag8[:].rearrange("p (b g) -> p b g", g=GB)[:, it][:, gl:gl + 1]
                    last = V.tensor_tensor_scan(zz[:, gl, 1:], d.broadcast_to([P, NCH - 1]), ww[:, gl, 0:NCH - 1], 0.0, ALU.mult, ALU.add)
                link(last)
                TT(ww[:], zz[:], rt[:, 0, :, 0:NCH], ALU.mult)
                TT(wt[:], zz[:], rt[:, 1, :, 0:NCH], ALU.mult).then_inc(state_done, 1)

            def y_du(q):
                dve.wait_ge(y_in[q], 32)
                V.scalar_tensor_tensor(yraw[:, q, :], uraw[:, q, :], dsk_s[:, q:q + 1], yraw[:, q, :], ALU.mult, ALU.add).then_inc(ydu, 1)

            def y_lo(q):
                dve.wait_ge(ysplit_hi, q + 1)
                TT(ylo[:, q, :], gt[:, q % 2, :], yhi[:, q, :].bitcast(F32), ALU.subtract).then_inc(ysplit, 1)

            def e1(it, last=False):
                b = B_E1 + 4 * it
                hi(b + 1, 1, HT, need=2 * b)
                hi(b + 2, 0, need=2 * (b + 1))
                rotate(it)
                gated(it, 0, b + 1)
                scan(it)
                hi(b + 3, 1, HT, need=2 * (b + 2))
                hi(b + 4, 0, need=2 * (b + 3))
                if last:
                    y_du(0)
                    y_du(1)
                gated(it, 1, b + 3)

            hi(B_E1 + 3, 1, HT, need=2 * (B_E1 + 2))
            rotate(0)
            gated(0, 0, B_E1 + 2)
            hi(B_E1 + 4, 0, need=2 * (B_E1 + 3))
            scan(0)
            gated(0, 1, B_E1 + 3)
            with dve.Fori(1, 3) as it:
                chain.enter(it - 1, 5)
                e1(it)
            chain.leave(2)
            e1(3, last=True)

            hi(B_E2 + 1, 1, need=G_E2)
            y_du(2)
            for q in range(HP - 1):
                y_lo(q)
            y_du(3)
            y_lo(3)

            def z_lo(k):
                dve.wait_ge(zs_hi, k + 1)
                TT(hlo[:, k, :], zt[:, k, :], hhi[:, k, :].bitcast(F32), ALU.subtract).then_inc(zs_lo, 1)

            def e2(m, first=False, last=False):
                if not first:
                    hi(B_E2 + 2 * m + 1, 1, need=G_E2 + 6 * m)
                hi(B_E2 + 2 * m + 2, 0, need=G_E2 + 6 * m + 2)
                if last:
                    for k in range(KC - 1):
                        z_lo(k)
                for h in range(2):
                    dve.wait_ge(sgt_done, 2 * m + h + 1)
                    dve.wait_ge(z_done, 2 * m + h + 1)
                    TT(t2[:, h, :], bank[2 + h][:], sg2[:, 2 + h, :], ALU.mult).then_inc(t2_done, 1)

            e2(0, first=True)
            with dve.Fori(1, KC - 1) as m:
                e2(m)
            e2(KC - 1, last=True)
            z_lo(KC - 1)

            with dve.Fori(0, KC // 2) as m2:
                for p in range(2):
                    hi(B_F + 2 * m2 + p + 1, (p + 1) % 2, need=G_F + 4 * m2 + 2 * p)
                    dve.wait_ge(xr_in[p], 16 * (m2 + 1))
                    for h in range(2):
                        dve.wait_ge(groups, G_F + 4 * m2 + 2 * p + h + 1)
                        TT(half(x1[:].rearrange("p (a b) t -> p b a t", b=2)[:, p, m2, :], h), bank[2 * p + h][:], half(xin[:, p, :], h),
                           ALU.add).then_inc(x1_done, 1)
            hi(B_G + 1, 1, need=G_G)
            norm(1, x1, gf, rs1, [sqb1[:, 0, :], hx1[:]])

            V.memset(gbuf[:, :, 0:2], 0.0).then_inc(pad_done, 1)
            dve.wait_ge(x1_out, 16 * KC)
            def ffn(f2, first=False):
                for p in range(2):
                    f, n, gr = 2 * f2 + p, B_G + 4 * f2 + 2 * p, G_G + 8 * f2 + 4 * p
                    w = cws[:].rearrange("p (a b) c -> p b a c", b=2)[:, p, f2, :]
                    if not (first and p == 0):
                        hi(n + 1, 1, need=gr)
                    hi(n + 2, 0, need=gr + 2)
                    dve.wait_ge(gcopy, 2 * f + 2 + 4)
                    dve.wait_ge(ff_done, 2 * f + 4)
                    link(V.tensor_scalar(cv[:], gbuf[:, p, 2:], w[:, 2:3], w[:, 3:4], ALU.mult, ALU.add))
                    link(V.scalar_tensor_tensor(cv[:], gbuf[:, p, 1:T + 1], w[:, 1:2], cv[:], ALU.mult, ALU.add))
                    V.scalar_tensor_tensor(cv[:], gbuf[:, p, 0:T], w[:, 0:1], cv[:], ALU.mult, ALU.add).then_inc(cv_done, 1)
                    dve.wait_ge(gelu_done, f + 1)
                    for h in range(2):
                        dve.wait_ge(groups, gr + 2 + h + 1)
                        TT(half(ff[:].rearrange("p (a b) t -> p b a t", b=2)[:, p, f2, :], h), half(cv[:], h), bank[4 * p + 2 + h][:],
                           ALU.mult).then_inc(ff_done, 1)

            ffn(0, first=True)
            with dve.Fori(1, NF // 2) as f2:
                chain.enter(f2 - 1, 4)
                ffn(f2)
            chain.leave(NF // 2 - 1)

            def fsplit(idx, j2, c, first=False):
                if not first:
                    dve.wait_ge((down_used, groups)[c], idx + (0, G_D)[c])
                src = ff[:].rearrange("p (a b) t -> p b a t", b=2)[:, c, j2, :]
                link(V.tensor_copy(fhi[:, c, :], src))
                TT(flo[:, c, :], src, fhi[:, c, :].bitcast(F32), ALU.subtract).then_inc(fs_lo, 1)

            def down(idx, j2, par):
                hi(B_D + idx + 1, par, need=G_D + idx)
                for c in range(2):
                    fsplit(idx + 1, j2, c)

            dve.wait_ge(groups, G_D)
            dve.wait_ge(ff_done, 2 * NF + 4)
            for c in range(2):
                fsplit(0, 0, c, first=True)
            for mh in range(2):
                i0 = 11 * mh
                with dve.Fori(0, 5) as j:
                    chain.enter(j, 4)
                    for q in range(2):
                        down(i0 + 2 * j + q, 2 * j + q + 1, (mh + q + 1) % 2)
                chain.leave(5)
                if mh == 0:
                    hi(B_D + 11, 1, need=G_D + 10)
                    fsplit(11, 0, 0)
                    dve.wait_ge(x1r_in, 16 * KC)
                for m in range(4):
                    if m < 3:
                        dve.wait_ge(tile_done, 3 * mh + m + 1)
                    else:
                        dve.wait_ge(groups, G_D + i0 + 11)
                    for h in range(2):
                        if mh:
                            dve.wait_ge(out_done, 64)
                        TT(half(osb[:, m, :], h), bank[2 * m + h][:], half(x1r[:, 4 * mh + m, :], h), ALU.add).then_inc(out_ready, 1)
                if mh == 0:
                    fsplit(11, 0, 1)


def bias_tables():
    i = np.arange(1, NPAT * HEADS + 1, dtype=np.float32)
    slopes = np.exp2(-8.0 * i / (NPAT * HEADS)).astype(np.float32).reshape(HEADS, NPAT).T
    q, k = np.arange(P)[:, None], np.arange(2 * P)[None, :]
    delta = q + P - k
    out = np.empty((NPAT, HEADS, P, 2 * P), np.float32)
    for g, dil in enumerate(DIL):
        valid = (delta >= 0) & (delta <= REACH)
        if T // dil < P:
            n = T // dil
            valid &= (k >= P) & (q // n == (k - P) // n)
        for h in range(HEADS):
            out[g, h] = np.where(valid, -slopes[g, h] * (delta * dil).astype(np.float32), np.float32(NEG))
    return np.ascontiguousarray(out.reshape(NPAT, HP, 2, P, 2 * P).transpose(0, 1, 3, 2, 4))


def blocks(w):
    k, m = w.shape
    return w.reshape(k // P, P, m // P, P).transpose(2, 1, 0, 3).reshape(m // P, P, k)


def kernel(**inputs):
    import concourse.bacc as bacc
    from concourse.bass_utils import run_bass_kernel_spmd

    a = {k: np.asarray(v) for k, v in inputs.items()}
    w_in = a["w_in"][0]
    aw = NPAT * HEADS * DH
    u_b = blocks(w_in[:, :SSM_W])
    qkv = blocks(w_in[:, SSM_W:SSM_W + 3 * aw]).reshape(3, NPAT, HP, P, D)
    ga = blocks(w_in[:, SSM_W + 3 * aw:SSM_W + 3 * aw + D])
    gb = blocks(w_in[:, SSM_W + 3 * aw + D:])
    vg = np.concatenate([blocks(a["glu_w_val"][0]), blocks(a["glu_w_gate"][0])], axis=2)
    fg, fu = blocks(a["ffn_w_gate"][0]), blocks(a["ffn_w_up"][0])
    wd = a["ffn_w_down"][0].reshape(NF // 2, 2, P, 2, HT).transpose(3, 0, 2, 1, 4).reshape(NF, P, 2 * HT)

    stream = [*qkv[:, 0, 0]]
    for hp in range(HP - 1):
        stream += [*qkv[:, 1, hp], *qkv[:, 2, hp], u_b[hp], *qkv[:, 0, hp + 1]]
    stream += [*qkv[:, 1, HP - 1], *qkv[:, 2, HP - 1], u_b[HP - 1]]
    stream += [*gb]
    for m in range(KC):
        stream += [ga[m], vg[m]]
    stream += [*blocks(a["w_out"][0])]
    for f in range(NF):
        stream += [fg[f], fu[f]]
    stream += [*wd]

    def cols(v):
        return v.reshape(-1, P).T

    def by_state(x, y):
        return np.concatenate([x.swapaxes(0, 1), y.swapaxes(0, 1)], axis=0)

    lam_re, lam_im, log_dt = a["ssm_lambda_re"][0], a["ssm_lambda_im"][0], a["ssm_log_dt"][0]
    b_re, b_im = a["ssm_b_re"][0], a["ssm_b_im"][0]
    c_re, c_im = (a[x][0].swapaxes(1, 2) for x in ("ssm_c_re", "ssm_c_im"))
    small = np.zeros((P, 3), np.float32)
    small[:NST, 0], small[NST:, 0], small[:NST, 1], small[NST:, 1], small[:, 2] = -1, 1, 1, -1, EPS
    eye = np.eye(P, dtype=np.float32)
    blk = np.kron(np.eye(2, dtype=np.float32), np.ones((DH, DH), np.float32))
    arrays = {
        "xT": a["x"][0].T.reshape(KC, P, T),
        "wblocks": np.stack(stream),
        "wup": blocks(a["w_attn_up"][0]),
        "masks": bias_tables(),
        "consts": np.stack([eye, blk, np.ones((P, P), np.float32)], axis=1),
        "gmix": cols(a["norm_mix_g"][0]),
        "gffn": cols(a["norm_ffn_g"][0]),
        "gqk": np.stack([np.tile(a[x][0], 2) for x in ("q_norm_g", "k_norm_g")], axis=1),
        "lam": np.stack([by_state(lam_re, lam_re), by_state(lam_im, lam_im),
                         np.broadcast_to(log_dt, (P, NGROUP))], axis=1),
        "bmat": np.stack([by_state(b_re, b_im), by_state(b_im, b_re)], axis=1),
        "cmat": np.stack([by_state(c_re, c_im), by_state(c_im, c_re)], axis=1),
        "dsk": cols(a["ssm_d"][0]),
        "cw": np.concatenate([a["ffn_conv_w"][0], a["ffn_conv_b"]], axis=0).T.reshape(NF, P, 4).transpose(1, 0, 2),
        "smallc": small,
    }
    nc = bacc.Bacc("TRN2", target_bir_lowering=False, num_devices=1)
    aps, feed = [], {}
    for name, v in arrays.items():
        v = np.ascontiguousarray(v)
        feed[f"in_{name}"] = v
        aps.append(nc.dram_tensor(f"in_{name}", v.shape, F32, kind="ExternalInput").ap())
    aps.append(nc.dram_tensor("out_t", (KC, P, T), F32, kind="ExternalOutput").ap())
    bass_hybrid_block(nc, *aps)
    r = run_bass_kernel_spmd(nc, [feed], core_ids=[0])
    return np.ascontiguousarray(r.results[0]["out_t"].reshape(D, T).T).reshape(1, T, D)
```
